# Optimizing a Trainium2 kernel written in Bass

```python
import math
import jax, jax.numpy as jnp
from jax import lax
import numpy as np

D_MODEL = 1024
BATCH = 1
SEQ = 256
DEPTH = 2

N_HEADS = 16
HEAD_DIM = D_MODEL // N_HEADS
CONV_WIDTH = 31
D_FF = ((8 * D_MODEL // 3) + 127) // 128 * 128
N_EXPERTS = 8
TOP_K = 2
Q_BLOCK = 128
EPS = 1e-6
N_A_LAYERS = (DEPTH + 1) // 2
N_B_LAYERS = DEPTH - N_A_LAYERS
N_DENSE = (DEPTH + 1) // 2
N_MOE = DEPTH // 2
FORGET_BIAS_MEAN = 2.0


def rms_norm(x, g):
    xf = x.astype(jnp.float32)
    y = xf * lax.rsqrt(jnp.mean(xf * xf, axis=-1, keepdims=True) + EPS)
    return (y * g.astype(jnp.float32)).astype(x.dtype)

def layer_norm(x, g, b):
    xf = x.astype(jnp.float32)
    mu = jnp.mean(xf, axis=-1, keepdims=True)
    var = jnp.mean(jnp.square(xf - mu), axis=-1, keepdims=True)
    y = (xf - mu) * lax.rsqrt(var + EPS)
    return (y * g.astype(jnp.float32) + b.astype(jnp.float32)).astype(x.dtype)

def conformer_conv(h, w_in, b_in, w_dw, b_dw, ln_g, ln_b, w_out, b_out):
    u = h @ w_in + b_in
    a, gate = jnp.split(u, 2, axis=-1)
    u = a * jax.nn.sigmoid(gate)
    u = lax.conv_general_dilated(
        u, w_dw[:, None, :].astype(u.dtype),
        window_strides=(1,), padding=[(CONV_WIDTH - 1, 0)],
        dimension_numbers=("NWC", "WIO", "NWC"),
        feature_group_count=D_MODEL) + b_dw
    u = layer_norm(u, ln_g, ln_b)
    u = jax.nn.silu(u)
    return u @ w_out + b_out

def swiglu(h, w_gate, w_up, w_down):
    return (jax.nn.silu(h @ w_gate) * (h @ w_up)) @ w_down

def moe_swiglu(h, router_w, router_b, w_gate, w_up, w_down):
    logits = (h @ router_w + router_b).astype(jnp.float32)
    top_vals, top_idx = lax.top_k(logits, TOP_K)
    top_p = jax.nn.softmax(top_vals, axis=-1)
    gates = jnp.sum(jax.nn.one_hot(top_idx, N_EXPERTS, dtype=jnp.float32) * top_p[..., None], axis=-2)
    gates = gates.astype(h.dtype)
    out = jnp.zeros_like(h)
    for e in range(N_EXPERTS):
        out = out + gates[..., e:e + 1] * swiglu(h, w_gate[e], w_up[e], w_down[e])
    return out

def shared_kv(x, kv_norm, w_kvf, b_f):
    bsz, seq, _ = x.shape
    hn = rms_norm(x, kv_norm)
    proj = hn @ w_kvf
    k = proj[..., :D_MODEL].reshape(bsz, seq, N_HEADS, HEAD_DIM)
    v = proj[..., D_MODEL:2 * D_MODEL].reshape(bsz, seq, N_HEADS, HEAD_DIM)
    f_logit = proj[..., 2 * D_MODEL:].astype(jnp.float32) + b_f.astype(jnp.float32)
    logf_cum = jnp.cumsum(jax.nn.log_sigmoid(f_logit), axis=1)
    return k, v, jnp.transpose(logf_cum, (0, 2, 1))

def forgetting_attention(q, k, v, logf_cum):
    seq = q.shape[1]
    scale = HEAD_DIM ** -0.5
    qf = q.astype(jnp.float32)
    kf = k.astype(jnp.float32)
    outs = []
    for blk in range(seq // Q_BLOCK):
        q0 = blk * Q_BLOCK
        q1 = q0 + Q_BLOCK
        s = jnp.einsum("bqhd,bkhd->bhqk", qf[:, q0:q1], kf[:, :q1]) * scale
        s = s + logf_cum[:, :, q0:q1, None] - logf_cum[:, :, None, :q1]
        mask = (q0 + jnp.arange(Q_BLOCK))[:, None] >= jnp.arange(q1)[None, :]
        s = jnp.where(mask, s, -jnp.inf)
        p = jax.nn.softmax(s, axis=-1).astype(v.dtype)
        outs.append(jnp.einsum("bhqk,bkhd->bqhd", p, v[:, :q1]))
    return jnp.concatenate(outs, axis=1)

def first_inputs(seed: int = 0) -> dict:
    key = jax.random.key(seed)
    ks = jax.random.split(key, 32)
    f32 = jnp.float32

    def w(k, shape, fan_in):
        return jax.random.normal(k, shape, f32) * (fan_in ** -0.5)

    def gain(k, shape):
        return 1.0 + 0.02 * jax.random.normal(k, shape, f32)

    def bias(k, shape, scale=0.02):
        return scale * jax.random.normal(k, shape, f32)

    D = D_MODEL
    return {
        "x": jax.random.normal(ks[0], (BATCH, SEQ, D), f32),
        "mix_norm": gain(ks[1], (DEPTH, D)),
        "ffn_norm": gain(ks[2], (DEPTH, D)),
        "conv_w_in": w(ks[3], (N_A_LAYERS, D, 2 * D), D),
        "conv_b_in": bias(ks[4], (N_A_LAYERS, 2 * D)),
        "conv_w_dw": w(ks[5], (N_A_LAYERS, CONV_WIDTH, D), CONV_WIDTH),
        "conv_b_dw": bias(ks[6], (N_A_LAYERS, D)),
        "conv_ln_g": gain(ks[7], (N_A_LAYERS, D)),
        "conv_ln_b": bias(ks[8], (N_A_LAYERS, D)),
        "conv_w_out": w(ks[9], (N_A_LAYERS, D, D), D),
        "conv_b_out": bias(ks[10], (N_A_LAYERS, D)),
        "kv_norm": gain(ks[11], (D,)),
        "w_kvf": w(ks[12], (D, 2 * D + N_HEADS), D),
        "b_f": FORGET_BIAS_MEAN + 0.5 * jax.random.normal(ks[13], (N_HEADS,), f32),
        "w_q": w(ks[14], (N_B_LAYERS, D, D), D),
        "w_o": w(ks[15], (N_B_LAYERS, D, D), D),
        "ffn_w_gate": w(ks[16], (N_DENSE, D, D_FF), D),
        "ffn_w_up": w(ks[17], (N_DENSE, D, D_FF), D),
        "ffn_w_down": w(ks[18], (N_DENSE, D_FF, D), D_FF),
        "router_w": w(ks[19], (N_MOE, D, N_EXPERTS), D),
        "router_b": bias(ks[20], (N_MOE, N_EXPERTS), 0.01),
        "moe_w_gate": w(ks[21], (N_MOE, N_EXPERTS, D, D_FF), D),
        "moe_w_up": w(ks[22], (N_MOE, N_EXPERTS, D, D_FF), D),
        "moe_w_down": w(ks[23], (N_MOE, N_EXPERTS, D_FF, D), D_FF),
        "final_norm": gain(ks[24], (D,)),
    }

def first_block(x, mix_norm, ffn_norm, conv_w_in, conv_b_in, conv_w_dw, conv_b_dw, conv_ln_g, conv_ln_b,
              conv_w_out, conv_b_out, kv_norm, w_kvf, b_f, w_q, w_o, ffn_w_gate, ffn_w_up, ffn_w_down,
              router_w, router_b, moe_w_gate, moe_w_up, moe_w_down, final_norm):
    bsz, seq, _ = x.shape
    a_i = b_i = d_i = m_i = 0
    k = v = logf_cum = None
    for layer in range(DEPTH):
        h = rms_norm(x, mix_norm[layer])
        if layer < N_A_LAYERS:
            x = x + conformer_conv(h, conv_w_in[a_i], conv_b_in[a_i], conv_w_dw[a_i], conv_b_dw[a_i],
                                   conv_ln_g[a_i], conv_ln_b[a_i], conv_w_out[a_i], conv_b_out[a_i])
            a_i += 1
        else:
            if k is None:
                k, v, logf_cum = shared_kv(x, kv_norm, w_kvf, b_f)
            q = (h @ w_q[b_i]).reshape(bsz, seq, N_HEADS, HEAD_DIM)
            o = forgetting_attention(q, k, v, logf_cum).reshape(bsz, seq, D_MODEL)
            x = x + o @ w_o[b_i]
            b_i += 1
        h = rms_norm(x, ffn_norm[layer])
        if layer % 2 == 0:
            x = x + swiglu(h, ffn_w_gate[d_i], ffn_w_up[d_i], ffn_w_down[d_i])
            d_i += 1
        else:
            x = x + moe_swiglu(h, router_w[m_i], router_b[m_i], moe_w_gate[m_i], moe_w_up[m_i], moe_w_down[m_i])
            m_i += 1
    return rms_norm(x, final_norm)


DEPTH_2 = 1

HEAD_DIM_2 = 64
MIX_WIDTH = D_MODEL
ATT_HEADS = 8
GDN_HEADS = 8
ATT_WIDTH = ATT_HEADS * HEAD_DIM_2
GDN_WIDTH = GDN_HEADS * HEAD_DIM_2
MOBA_BLOCK = 256
MOBA_TOPK = 3
MOBA_QCHUNK = 32
GDN_CHUNK = 64
CONV_WIDTH_2 = 4
D_FF_2 = 4 * D_MODEL
REL_BUCKETS = 32
REL_MAX_EXACT = 16
REL_MAX_DIST = 128
IN_SIZES = [ATT_WIDTH, ATT_WIDTH, ATT_WIDTH, 3 * GDN_WIDTH, GDN_WIDTH, GDN_HEADS, GDN_HEADS]
IN_COLS = sum(IN_SIZES)


def rms_norm_2(x, w):
    xf = x.astype(jnp.float32)
    y = xf * lax.rsqrt(jnp.mean(xf * xf, axis=-1, keepdims=True) + EPS)
    return (y * w.astype(jnp.float32)).astype(x.dtype)

def l2_normalize(x):
    xf = x.astype(jnp.float32)
    return xf * lax.rsqrt(jnp.sum(xf * xf, axis=-1, keepdims=True) + EPS)

def rel_bucket(dist):
    d = jnp.maximum(dist, 0)
    large = REL_MAX_EXACT + (
        jnp.log(jnp.maximum(d, 1).astype(jnp.float32) / REL_MAX_EXACT)
        / math.log(REL_MAX_DIST / REL_MAX_EXACT)
        * (REL_BUCKETS - REL_MAX_EXACT)
    ).astype(jnp.int32)
    large = jnp.minimum(large, REL_BUCKETS - 1)
    return jnp.where(d < REL_MAX_EXACT, d, large)

def moba_attention(q, k, v, rel_bias):
    B, S, H, dh = q.shape
    nb = -(-S // MOBA_BLOCK)
    s_pad = nb * MOBA_BLOCK
    qh = q.transpose(0, 2, 1, 3)
    pad = ((0, 0), (0, 0), (0, s_pad - S), (0, 0))
    kh = jnp.pad(k.transpose(0, 2, 1, 3), pad)
    vh = jnp.pad(v.transpose(0, 2, 1, 3), pad)
    kb = kh.reshape(B, H, nb, MOBA_BLOCK, dh)
    vb = vh.reshape(B, H, nb, MOBA_BLOCK, dh)
    kmean = jnp.mean(kb.astype(jnp.float32), axis=3)
    rel_bias = rel_bias.astype(jnp.float32)

    gate = jnp.einsum('bhsd,bhnd->bhsn', qh.astype(jnp.float32), kmean)
    pos = jnp.arange(S)
    n_past = pos // MOBA_BLOCK
    past = jnp.arange(nb)[None, :] < n_past[:, None]
    gate = jnp.where(past, gate, -jnp.inf)
    kk = min(MOBA_TOPK, nb)
    _, sel = lax.top_k(gate, kk)
    sel_valid = jnp.arange(kk)[None, :] < jnp.minimum(n_past, MOBA_TOPK)[:, None]

    nc = S // MOBA_QCHUNK
    q_c = qh.reshape(B, H, nc, MOBA_QCHUNK, dh).transpose(2, 0, 1, 3, 4)
    sel_c = sel.reshape(B, H, nc, MOBA_QCHUNK, kk).transpose(2, 0, 1, 3, 4)
    valid_c = sel_valid.reshape(nc, MOBA_QCHUNK, kk)
    scale = HEAD_DIM_2 ** -0.5
    off = jnp.arange(MOBA_BLOCK)
    head_idx = jnp.arange(H)[:, None, None, None]
    gather_blocks = jax.vmap(jax.vmap(lambda blocks, idx: blocks[idx]))

    def chunk_fn(args):
        c, qc, sc, vc = args
        q0 = c * MOBA_QCHUNK
        qpos = q0 + jnp.arange(MOBA_QCHUNK)
        own = q0 // MOBA_BLOCK
        k_own = lax.dynamic_slice_in_dim(kb, own, 1, axis=2)[:, :, 0]
        v_own = lax.dynamic_slice_in_dim(vb, own, 1, axis=2)[:, :, 0]
        d_own = qpos[:, None] - (own * MOBA_BLOCK + off)[None, :]
        l_own = jnp.einsum('bhqd,bhkd->bhqk', qc, k_own).astype(jnp.float32) * scale
        l_own = l_own + rel_bias[:, rel_bucket(d_own)]
        l_own = jnp.where(d_own >= 0, l_own, -jnp.inf)
        k_sel = gather_blocks(kb, sc)
        v_sel = gather_blocks(vb, sc)
        d_sel = qpos[:, None, None] - (sc[..., None] * MOBA_BLOCK + off)
        l_sel = jnp.einsum('bhqd,bhqnkd->bhqnk', qc, k_sel).astype(jnp.float32) * scale
        l_sel = l_sel + rel_bias[head_idx, rel_bucket(d_sel)]
        l_sel = jnp.where(vc[:, :, None], l_sel, -jnp.inf)
        logits = jnp.concatenate(
            [l_own, l_sel.reshape(B, H, MOBA_QCHUNK, kk * MOBA_BLOCK)], axis=-1)
        p = jax.nn.softmax(logits, axis=-1)
        p_own = p[..., :MOBA_BLOCK].astype(v.dtype)
        p_sel = p[..., MOBA_BLOCK:].reshape(B, H, MOBA_QCHUNK, kk, MOBA_BLOCK).astype(v.dtype)
        return (jnp.einsum('bhqk,bhkd->bhqd', p_own, v_own)
                + jnp.einsum('bhqnk,bhqnkd->bhqd', p_sel, v_sel))

    o = lax.map(chunk_fn, (jnp.arange(nc), q_c, sel_c, valid_c))
    return o.transpose(1, 0, 3, 2, 4).reshape(B, S, H * dh)

def causal_depthwise_conv_silu(x, w):
    C = x.shape[-1]
    y = lax.conv_general_dilated(
        x, w[:, None, :].astype(x.dtype), window_strides=(1,),
        padding=[(CONV_WIDTH_2 - 1, 0)], dimension_numbers=('NWC', 'WIO', 'NWC'),
        feature_group_count=C)
    return jax.nn.silu(y)

def gated_deltanet(qkv, z, a, b, conv_w, A_log, dt_bias, norm_w):
    B, S, _ = qkv.shape
    H, dh, C = GDN_HEADS, HEAD_DIM_2, GDN_CHUNK
    nc = S // C
    qkv = causal_depthwise_conv_silu(qkv, conv_w)
    q, k, v = jnp.split(qkv, 3, axis=-1)
    q = l2_normalize(q.reshape(B, S, H, dh)) * (dh ** -0.5)
    k = l2_normalize(k.reshape(B, S, H, dh))
    v = v.reshape(B, S, H, dh).astype(jnp.float32)
    beta = jax.nn.sigmoid(b.astype(jnp.float32))
    g = -jnp.exp(A_log.astype(jnp.float32)) * jax.nn.softplus(
        a.astype(jnp.float32) + dt_bias.astype(jnp.float32))

    def to_chunks(t):
        t = jnp.moveaxis(t, 2, 1)
        return t.reshape((B, H, nc, C) + t.shape[3:])

    qc, kc, vc = to_chunks(q), to_chunks(k), to_chunks(v)
    bc = to_chunks(beta)
    g_cum = jnp.cumsum(to_chunks(g), axis=-1)
    causal = jnp.tril(jnp.ones((C, C), dtype=bool))
    strict = jnp.tril(jnp.ones((C, C), dtype=bool), k=-1)
    decay = jnp.exp(jnp.where(causal, g_cum[..., :, None] - g_cum[..., None, :], -jnp.inf))
    k_beta = kc * bc[..., None]
    m = jnp.where(strict, jnp.einsum('bhnid,bhnjd->bhnij', k_beta, kc) * decay, 0.0)
    a_mat = m + jnp.eye(C, dtype=jnp.float32)
    rhs = jnp.concatenate([vc * bc[..., None], k_beta * jnp.exp(g_cum)[..., None]], axis=-1)
    uw = lax.linalg.triangular_solve(a_mat, rhs, left_side=True, lower=True, unit_diagonal=True)
    u, w = uw[..., :dh], uw[..., dh:]
    attn_intra = jnp.einsum('bhnid,bhnjd->bhnij', qc, kc) * decay
    q_dec = qc * jnp.exp(g_cum)[..., None]
    k_dec = kc * jnp.exp(g_cum[..., -1:] - g_cum)[..., None]
    g_last = jnp.exp(g_cum[..., -1])

    def step(state, xs):
        u_c, w_c, q_c, k_c, a_c, gl = xs
        v_new = u_c - jnp.einsum('bhck,bhkv->bhcv', w_c, state)
        o = jnp.einsum('bhck,bhkv->bhcv', q_c, state) + jnp.einsum('bhcs,bhsv->bhcv', a_c, v_new)
        state = state * gl[..., None, None] + jnp.einsum('bhck,bhcv->bhkv', k_c, v_new)
        return state, o

    xs = tuple(jnp.moveaxis(t, 2, 0) for t in (u, w, q_dec, k_dec, attn_intra, g_last))
    state0 = jnp.zeros((B, H, dh, dh), dtype=jnp.float32)
    _, o = lax.scan(step, state0, xs)
    o = jnp.moveaxis(o, 0, 2).reshape(B, H, S, dh).transpose(0, 2, 1, 3)
    o = o * lax.rsqrt(jnp.mean(o * o, axis=-1, keepdims=True) + EPS) * norm_w.astype(jnp.float32)
    o = o * jax.nn.silu(z.reshape(B, S, H, dh).astype(jnp.float32))
    return o.reshape(B, S, GDN_WIDTH).astype(qkv.dtype)

def second_inputs(seed: int = 0) -> dict:
    key = jax.random.key(seed)
    ks = jax.random.split(key, 16)
    f32 = jnp.float32
    x = jax.random.normal(ks[0], (BATCH, SEQ, D_MODEL), f32)
    w_in = jax.random.normal(ks[1], (DEPTH_2, D_MODEL, IN_COLS), f32) * D_MODEL ** -0.5
    w_out = jax.random.normal(ks[2], (DEPTH_2, MIX_WIDTH, D_MODEL), f32) * MIX_WIDTH ** -0.5
    conv_w = jax.random.normal(ks[3], (DEPTH_2, CONV_WIDTH_2, 3 * GDN_WIDTH), f32) * CONV_WIDTH_2 ** -0.5
    A_log = jnp.log(jax.random.uniform(ks[4], (DEPTH_2, GDN_HEADS), f32, 1.0, 16.0))
    dt = jnp.exp(jax.random.uniform(ks[5], (DEPTH_2, GDN_HEADS), f32, math.log(1e-3), math.log(1e-1)))
    dt_bias = dt + jnp.log(-jnp.expm1(-dt))
    gdn_norm_w = 1.0 + 0.05 * jax.random.normal(ks[6], (DEPTH_2, HEAD_DIM_2), f32)
    rel_bias = 0.5 * jax.random.normal(ks[7], (ATT_HEADS, REL_BUCKETS), f32)
    pre_mix_norm = 1.0 + 0.05 * jax.random.normal(ks[8], (DEPTH_2, D_MODEL), f32)
    post_mix_norm = 1.0 + 0.05 * jax.random.normal(ks[9], (DEPTH_2, D_MODEL), f32)
    pre_mlp_norm = 1.0 + 0.05 * jax.random.normal(ks[10], (DEPTH_2, D_MODEL), f32)
    post_mlp_norm = 1.0 + 0.05 * jax.random.normal(ks[11], (DEPTH_2, D_MODEL), f32)
    w_up = jax.random.normal(ks[12], (DEPTH_2, D_MODEL, D_FF_2), f32) * D_MODEL ** -0.5
    w_down = jax.random.normal(ks[13], (DEPTH_2, D_FF_2, D_MODEL), f32) * D_FF_2 ** -0.5
    return {"x": x, "w_in": w_in, "w_out": w_out, "conv_w": conv_w, "A_log": A_log,
            "dt_bias": dt_bias, "gdn_norm_w": gdn_norm_w, "rel_bias": rel_bias,
            "pre_mix_norm": pre_mix_norm, "post_mix_norm": post_mix_norm,
            "pre_mlp_norm": pre_mlp_norm, "post_mlp_norm": post_mlp_norm,
            "w_up": w_up, "w_down": w_down}

def second_block(x, w_in, w_out, conv_w, A_log, dt_bias, gdn_norm_w, rel_bias,
              pre_mix_norm, post_mix_norm, pre_mlp_norm, post_mlp_norm, w_up, w_down):
    B, S, _ = x.shape
    split_points = np.cumsum(IN_SIZES)[:-1].tolist()
    for l in range(DEPTH_2):
        h = rms_norm_2(x, pre_mix_norm[l])
        proj = jnp.einsum('bsd,dc->bsc', h, w_in[l])
        att_q, att_k, att_v, gdn_qkv, gdn_z, gdn_a, gdn_b = jnp.split(proj, split_points, axis=-1)
        o_att = moba_attention(att_q.reshape(B, S, ATT_HEADS, HEAD_DIM_2),
                               att_k.reshape(B, S, ATT_HEADS, HEAD_DIM_2),
                               att_v.reshape(B, S, ATT_HEADS, HEAD_DIM_2), rel_bias)
        o_gdn = gated_deltanet(gdn_qkv, gdn_z, gdn_a, gdn_b, conv_w[l], A_log[l],
                               dt_bias[l], gdn_norm_w[l])
        mix = jnp.einsum('bsc,cd->bsd', jnp.concatenate([o_att, o_gdn], axis=-1), w_out[l])
        x = x + rms_norm_2(mix, post_mix_norm[l])
        h = rms_norm_2(x, pre_mlp_norm[l])
        m = jnp.einsum('bsf,fd->bsd', jnp.square(jax.nn.relu(jnp.einsum('bsd,df->bsf', h, w_up[l]))), w_down[l])
        x = x + rms_norm_2(m, post_mlp_norm[l])
    return x


def setup_inputs(seed=0):
    out = dict(first_inputs(seed))
    for name, value in second_inputs(seed + 1).items():
        if name != "x":
            out[name + "_2"] = value
    return out


def reference(
    x, mix_norm, ffn_norm, conv_w_in, conv_b_in, conv_w_dw, conv_b_dw, conv_ln_g, conv_ln_b,
    conv_w_out, conv_b_out, kv_norm, w_kvf, b_f, w_q, w_o, ffn_w_gate, ffn_w_up, ffn_w_down,
    router_w, router_b, moe_w_gate, moe_w_up, moe_w_down, final_norm, w_in_2, w_out_2, conv_w_2,
    A_log_2, dt_bias_2, gdn_norm_w_2, rel_bias_2, pre_mix_norm_2, post_mix_norm_2,
    pre_mlp_norm_2, post_mlp_norm_2, w_up_2, w_down_2,
):
    x = first_block(
        x, mix_norm, ffn_norm, conv_w_in, conv_b_in, conv_w_dw, conv_b_dw, conv_ln_g, conv_ln_b,
        conv_w_out, conv_b_out, kv_norm, w_kvf, b_f, w_q, w_o, ffn_w_gate, ffn_w_up, ffn_w_down,
        router_w, router_b, moe_w_gate, moe_w_up, moe_w_down, final_norm,
    )
    return second_block(
        x, w_in_2, w_out_2, conv_w_2, A_log_2, dt_bias_2, gdn_norm_w_2, rel_bias_2,
        pre_mix_norm_2, post_mix_norm_2, pre_mlp_norm_2, post_mlp_norm_2, w_up_2, w_down_2,
    )


_drawn_inputs = setup_inputs


def setup_inputs(seed=0):
    import zlib

    import numpy as np

    out = dict(_drawn_inputs(seed))
    spreads = {}
    factors = {}
    for name, (base, spread) in spreads.items():
        noise = np.random.default_rng([zlib.crc32(name.encode()), seed]).standard_normal(out[name].shape)
        drawn = base * np.exp(spread * noise) if base else spread * noise
        out[name] = __import__('jax').numpy.asarray(drawn.astype(out[name].dtype))
    for name, factor in factors.items():
        out[name] = (out[name] * factor).astype(out[name].dtype)
    return out
```

```python
from contextlib import ExitStack

import numpy as np

import concourse.bass as bass
from concourse import mybir

F32 = mybir.dt.float32
I32 = mybir.dt.int32
F32R = mybir.dt.float32r
ALU = mybir.AluOpType
ACT = mybir.ActivationFunctionType
AX = mybir.AxisListType.X

P = 128
D = 1024
SEQ = 256
TT = SEQ // P
DC = D // P
EPS = 1e-6
NEG = -1e30

HEADS = 16
DH = 64
TAPS = 31
FF = 2816
FT = FF // P
EXPERTS = 8
ATT2 = 512
GH = 8
CHUNK = 64
TAPS2 = 4
FF2 = 4096
FT2 = FF2 // P
BUCKETS = 32
LEVELS = 6
CONV_DVE = 6

SLOTS = 6
UNIT = 4096
N_WIN, N_WOUT, N_GU, N_DOWN, N_Q, N_KV, N_O = 4, 2, 11, 6, 2, 4, 2
N_PRE = N_WIN + N_WOUT + N_GU + N_DOWN + N_Q + N_KV + N_O
PER_EXPERT = 17
RAW = 3
SPLIT = 3
HALF = UNIT // 2
HALVES = 33
PAIRED = 30
LOADS = PAIRED // 2 + HALVES - PAIRED
N_POST = 3 + 3 + 1 + 2 + 8 + 8
POST0 = N_PRE + EXPERTS * PER_EXPERT

CONST_NAMES = ["ident", "anti", "causal", "blockdecay", "before", "ones", "iota", "tri64", "all64"]
CONST = {n: i * P for i, n in enumerate(CONST_NAMES)}
LEVEL0 = len(CONST_NAMES) * P
IOTA8 = LEVEL0 + LEVELS * P
EPSCOL = IOTA8 + EXPERTS
HK = 384
N_CONST = EPSCOL + 1

VEC = {}
N_VEC = 0
for _name, _n in [("mix0", DC), ("ffn0", DC), ("mix1", DC), ("ffn1", DC), ("kv", DC), ("b_in", 2 * DC),
                  ("w_dw", TAPS * DC), ("b_dw", DC), ("ln_g", DC), ("ln_b", DC), ("pre_mix", DC),
                  ("pre_mlp", DC), ("conv2", TAPS2 * 12), ("b_f", 1), ("relb", GH)]:
    VEC[_name] = N_VEC
    N_VEC += _n
WF, WR, WAB = 0, DC * HEADS, DC * (HEADS + EXPERTS)
N_NARROW = DC * (HEADS + EXPERTS + 2 * GH)
R_RB, R_ALOG, R_DT, R_NORM = 0, 8, 16, 24
N_ROW = 24 + DH


def shape_constants():
    c = np.zeros((P, N_CONST), np.float32)
    p, f = np.arange(P)[:, None], np.arange(P)[None, :]
    same = p // CHUNK == f // CHUNK
    tables = {
        "ident": p == f,
        "anti": p + f == P - 1,
        "causal": np.where(f <= p, 0.0, NEG),
        "blockdecay": np.where(same & (p <= f), 0.0, NEG),
        "before": p < f,
        "ones": np.ones((P, P)),
        "iota": np.broadcast_to(f, (P, P)),
        "tri64": same & (p <= f),
        "all64": same,
    }
    for n, a in tables.items():
        c[:, CONST[n]:CONST[n] + P] = a
    for lv in range(LEVELS):
        size = 1 << lv
        c[:, LEVEL0 + lv * P:LEVEL0 + (lv + 1) * P] = (
            (p // (2 * size) == f // (2 * size)) & (p // size % 2 == 0) & (f // size % 2 == 1))
    c[:, IOTA8:IOTA8 + EXPERTS] = np.arange(EXPERTS)
    dist = SEQ - 1 - np.arange(HK)
    d = np.maximum(dist, 0)
    exact = BUCKETS // 2
    large = exact + (np.log(np.maximum(d, 1).astype(np.float32) / np.float32(exact))
                     / np.float32(np.log(128 / exact)) * np.float32(exact)).astype(np.int32)
    bucket = np.where(d < exact, d, np.minimum(large, BUCKETS - 1))
    bias = np.zeros((BUCKETS, 2 * HK), np.float32)
    bias[:, 0:HK] = (np.arange(BUCKETS)[:, None] == bucket) & (dist >= 0)
    bias[:, HK:] = np.where(dist >= 0, 0.0, NEG)
    c[:, EPSCOL] = EPS
    return c, bias


class Banks:

    def __init__(self, full, free):
        self.full, self.free, self.uses, self.at, self.next = full, free, [0] * 8, {}, 0

    def add(self, name):
        b = self.next
        self.at[name] = (b, self.uses[b])
        self.uses[b] += 1
        self.next = (b + 1) % 8


def build(nc, dr, out, dbg=None):
    with ExitStack() as ctx:
        def sb(name, cols, dt=F32):
            return ctx.enter_context(nc.sbuf_tensor(name, [P, cols], dt))

        sems = {}

        def S(name):
            if name not in sems:
                sems[name] = ctx.enter_context(nc.semaphore(name))
            return sems[name]

        def sb2(name, cols):
            with nc.sbuf_tensor(name, [P, cols], F32) as plain:
                pass
            return plain, sb(name + "_r", cols, F32R)

        with nc.sbuf_tensor("ring", [P, SLOTS * UNIT], F32) as ring:
            pass
        raw = sb("raw", RAW * UNIT)
        wh = sb("wh", SPLIT * HALF, F32R)
        wl = sb("wl", SPLIT * HALF, F32R)
        x_t = sb("x_t", TT * D)
        h_t = sb("h_t", TT * D)
        ht_t = sb("ht_t", DC * SEQ)
        big = sb("big", 8192)
        f1, f1_r = sb2("f1", 2048)
        f2, f2_r = sb2("f2", 2048)
        f3 = sb("f3", 2048)
        g1 = sb("g1", 2048)
        gb = sb("gb", 2 * D)
        cst = sb("cst", N_CONST)
        vec = sb("vec", N_VEC)
        nar = sb("nar", N_NARROW)
        row = sb("row", N_ROW)
        ss = sb("ss", 16)
        mid = sb("mid", 512)
        rt = sb("rt", 512)
        nit = sb("nit", 8, I32)
        ps = [ctx.enter_context(nc.psum_tensor(f"ps{b}", [P, 512], F32)) for b in range(8)]

        X = x_t[:, :].rearrange("p (t d) -> p t d", t=TT)
        H = h_t[:, :].rearrange("p (t d) -> p t d", t=TT)
        HT = ht_t[:, :].rearrange("p (c s) -> p c s", c=DC)
        F3c = f3[:, :].rearrange("p (c s) -> p c s", c=DC)

        def C(name, n=P):
            return cst[:, CONST[name]:CONST[name] + n]

        def V(name, i):
            return vec[:, VEC[name] + i:VEC[name] + i + 1]

        def slot(k):
            return ring[:, k * UNIT:(k + 1) * UNIT]

        pre = Banks([S(f"full{b}") for b in range(8)], [S(f"free{b}") for b in range(8)])
        post = Banks([S(f"full_b{b}") for b in range(8)], [S(f"free_b{b}") for b in range(8)])

        def plan_norm(B, u):
            for j in range(4):
                B.add(("T", u, j))

        def plan_attention(B, a, heads):
            for h in range(heads + 2):
                if h < heads:
                    B.add(("S", a, h))
                if 1 <= h <= heads:
                    B.add(("PT", a, h - 1))
                if h >= 2 and h % 2 == 0:
                    B.add(("O", a, (h - 2) // 2))

        def plan_four(B, name):
            for tt in range(TT):
                for c in range(2):
                    B.add((name, tt, c))

        plan_norm(pre, 0)
        for i in range(DC):
            pre.add(("gate", i))
            pre.add(("a", i))
        for i in range(CONV_DVE, DC):
            pre.add(("cv", i))
        pre.add(("mu",))
        pre.add(("var",))
        plan_four(pre, "wout")
        plan_norm(pre, 1)
        for i in range(FT):
            pre.add(("ffg", i))
            pre.add(("ffu", i))
        plan_four(pre, "ffd")
        plan_norm(pre, 2)
        for n in range(DC):
            pre.add(("q", n))
        for n in range(DC):
            pre.add(("k", n))
        plan_four(pre, "v")
        pre.add(("f",))
        plan_attention(pre, 0, HEADS)
        plan_four(pre, "wo")
        plan_norm(pre, 3)
        pre.add(("logits",))
        pre.add(("pos",))

        post.add(("hk",))
        plan_norm(post, 5)
        for n in range(4):
            post.add(("q2", n))
        for n in range(4):
            post.add(("k2", n))
        for tt in range(TT):
            post.add(("v2", tt))
        plan_attention(post, 1, GH)
        for n in range(12):
            post.add(("g", n))
        for tt in range(TT):
            post.add(("z", tt))
        post.add(("ab",))
        post.add(("gcum",))
        post.add(("gT",))
        for tt in range(TT):
            for j in range(3):
                post.add(("tm", tt, j))
        for tt in range(TT):
            for q in range(2):
                for n in ("KT", "KBT", "QT", "QDT"):
                    post.add((n, tt, q))
            for q in range(2):
                post.add(("DT", tt, q))
                post.add(("KK", tt, q))
                post.add(("QK", tt, q))
            for lv in range(LEVELS):
                for q in range(2):
                    post.add(("Z", tt, lv, q))
                for q in range(2):
                    post.add(("XZ", tt, lv, q))
                    post.add(("ZW", tt, lv, q))
            post.add(("U", tt))
            for q in range(2):
                post.add(("WT", tt, q))
        for c in range(4):
            post.add(("vn", c))
            post.add(("o", c))
            post.add(("st", c))
        for tt in range(TT):
            post.add(("og", tt))
        plan_four(post, "mix")
        plan_norm(post, 7)
        for i in range(FT2):
            post.add(("up", i))
        plan_four(post, "mlp")

        def opened(pe, B, name):
            b, k = B.at[name]
            if k:
                pe.wait_ge(B.free[b], k)
            return ps[b]

        def closed(B, name, ins):
            ins.then_inc(B.full[B.at[name][0]], 1)

        def filled(eng, B, name):
            b, k = B.at[name]
            eng.wait_ge(B.full[b], k + 1)
            return ps[b]

        def let_go(B, name, ins):
            b, k = B.at[name]
            ins.then_inc(B.free[b], 1)
            return B.free[b], k + 1

        class Chain:

            def __init__(self, eng, name):
                self.eng, self.sem, self.n = eng, S(name), 0

            def __call__(self, ins):
                self.n += 1
                ins.then_inc(self.sem, 1)
                self.eng.wait_ge(self.sem, self.n)

            def go(self, ins):
                self.n += 1
                ins.then_inc(self.sem, 1)

            def join(self, back=0):
                if self.n - back > 0:
                    self.eng.wait_ge(self.sem, self.n - back)

        AT = big[:, 0:FT2 * SEQ].rearrange("p (f s) -> p f s", s=SEQ)
        UPAD = SEQ + TAPS - 1
        U = big[:, 0:DC * UPAD].rearrange("p (c s) -> p c s", c=DC)
        CV = big[:, DC * UPAD:DC * UPAD + DC * SEQ].rearrange("p (c s) -> p c s", c=DC)
        SQ = f1[:, :].rearrange("p (c s) -> p c s", c=DC)
        CVB = f3[:, :].rearrange("p (c s) -> p c s", c=DC)
        MUV = f2[:, 0:SEQ]
        SIG = f2[:, SEQ:3 * SEQ].rearrange("p (b s) -> p b s", b=2)
        FFG = f2[:, 0:2 * SEQ].rearrange("p (b s) -> p b s", b=2)
        DIAG = ([f1[:, t * P:(t + 1) * P] for t in range(16)] + [h_t[:, t * P:(t + 1) * P] for t in range(16)]
                + [big[:, 8192 - (t + 1) * P:8192 - t * P] for t in range(30)])
        assert DC * (UPAD + SEQ) + 30 * P <= 8192 and len(DIAG) == (DC - CONV_DVE) * TAPS
        QZ = big[:, 0:HEADS * SEQ].rearrange("p (h s) -> p h s", s=SEQ)
        PR = big[:, 4096:4096 + 768].rearrange("p (b n) -> p b n", b=2)
        PT = big[:, 4864:4864 + 768].rearrange("p (b n) -> p b n", b=2)
        NL = big[:, 5632:5632 + SEQ]
        FA = big[:, 5888:5888 + 4 * SEQ].rearrange("p (b s) -> p b s", b=4)
        KT = f1[:, :].rearrange("p (c s) -> p c s", s=SEQ)
        HKB = big[:, 2048:4096].rearrange("p (h s) -> p h s", s=SEQ)
        HTGH = f1_r[:, 0:1024].rearrange("p (c s) -> p c s", s=P)
        HTGL = f1_r[:, 1024:2048].rearrange("p (c s) -> p c s", s=P)
        HTn = big[:, 1024:2048].rearrange("p (c s) -> p c s", s=P)
        SG = big[:, 2048:3072].rearrange("p (b n) -> p b n", b=2)
        PRD = big[:, 3072:4096].rearrange("p (b n) -> p b n", b=2)
        ATEH = f2_r[:, 0:1024].rearrange("p (b n) -> p b n", b=2)
        ATEL = f2_r[:, 1024:2048].rearrange("p (b n) -> p b n", b=2)
        YS = big[:, 5120:6144]
        PG = big[:, 6144:6400].rearrange("p (t s) -> p t s", t=TT)
        PX = big[:, 6400:6656].rearrange("p (t s) -> p t s", t=TT)
        PTX = big[:, 6656:6912]
        GS = big[:, 6912:6913]
        CP = big[:, 6920:6924]
        POSI = rt[:, 0:24].rearrange("p (t i) -> p t i", t=TT)
        GATI = rt[:, 24:48].rearrange("p (t i) -> p t i", t=TT)
        UP2 = SEQ + TAPS2 - 1
        GU_ = big[:, 0:12 * UP2].rearrange("p (c s) -> p c s", c=12)
        GF = big[:, 3200:3200 + 12 * SEQ].rearrange("p (c s) -> p c s", c=12)
        TM = big[:, 0:3072].rearrange("p (t j n) -> p t j n", t=TT, j=3)
        KB = h_t[:, 0:1024].rearrange("p (t n) -> p t n", t=TT)
        QD = h_t[:, 1024:2048].rearrange("p (t n) -> p t n", t=TT)
        RW = f1[:, 0:1024].rearrange("p (t n) -> p t n", t=TT)
        VB = f1[:, 1024:2048].rearrange("p (t n) -> p t n", t=TT)
        KD = f2[:, 0:1024].rearrange("p (t n) -> p t n", t=TT)
        ZS = f2[:, 1024:2048].rearrange("p (t n) -> p t n", t=TT)
        QDT = ht_t[0:DH, :].rearrange("p (h s) -> p h s", s=SEQ)
        ATG = g1[:, :].rearrange("p (t h s) -> p t h s", t=TT, h=GH)
        MT = big[:, 0:1024]
        XI = big[:, 1024:2048]
        WI = big[:, 2048:3072]
        KTt = big[0:DH, 3072:4096].rearrange("p (h s) -> p h s", s=P)
        KBTt = big[0:DH, 4096:5120].rearrange("p (h s) -> p h s", s=P)
        QTt = big[0:DH, 5120:6144].rearrange("p (h s) -> p h s", s=P)
        ZI = big[:, 6144:7168]
        CI = big[:, 7168:8192]
        DTs = ZI
        QN = [TM[:, 0, 0, :], g1[:, 1024:1536]]
        KN = [TM[:, 0, 1, :], g1[:, 1536:2048]]
        UU = h_t[:, 0:1024].rearrange("p (t n) -> p t n", t=TT)
        WT = [f3[0:DH, 1024:2048].rearrange("p (h s) -> p h s", s=P),
              h_t[0:DH, 1024:2048].rearrange("p (h s) -> p h s", s=P)]
        VN = [big[:, 0:512], big[:, 512:1024]]
        ST = big[0:DH, 3072:3584].rearrange("p (h v) -> p h v", v=DH)
        STT_ = big[0:DH, 3584:4096].rearrange("p (h v) -> p h v", v=DH)
        OG = big[:, 4096:5120].rearrange("p (t n) -> p t n", t=TT)
        OSQ = big[:, 5120:6144].rearrange("p (t n) -> p t n", t=TT)
        M2 = h_t[:, :].rearrange("p (t d) -> p t d", t=TT)
        BETA = mid[:, 0:16].rearrange("p (t h) -> p t h", t=TT)
        GLOG = mid[:, 16:32].rearrange("p (t h) -> p t h", t=TT)
        GC = mid[:, 32:48].rearrange("p (t h) -> p t h", t=TT)
        NGC = mid[:, 48:64].rearrange("p (t h) -> p t h", t=TT)
        EG = mid[:, 64:80].rearrange("p (t h) -> p t h", t=TT)
        EGL = mid[:, 80:96].rearrange("p (t h) -> p t h", t=TT)
        SC2 = mid[:, 96:128].rearrange("p (j t h) -> p j t h", j=2, t=TT)
        GLAST = mid[:, 128:160].rearrange("p (c h) -> p c h", c=4)
        TMP = [mid[:, 160 + 16 * i:176 + 16 * i].rearrange("p (t h) -> p t h", t=TT) for i in range(5)]
        GTR = mid[0:GH, 240:240 + SEQ]

        block = ctx.enter_context(nc.Block())

        @block.sync
        def _(sp):
            sp.dma_start(X, dr["x"].rearrange("(t p) d -> p t d", p=P)).then_inc(S("ld_x"), 16)
            sp.dma_start(cst[:, :], dr["const"]).then_inc(S("ld_const"), 16)
            sp.dma_start(vec[:, :], dr["vec"]).then_inc(S("ld_vec"), 16)
            sp.dma_start(nar[:, :], dr["narrow"]).then_inc(S("ld_narrow"), 16)
            sp.dma_start(row[:, :], dr["rows"].partition_broadcast(P)).then_inc(S("ld_row"), 16)
            sp.dma_start(gb[:, 0:D], dr["gains"][0, :].partition_broadcast(P)).then_inc(S("ld_gb0"), 16)
            sp.dma_start(gb[:, D:2 * D], dr["gains"][1, :].partition_broadcast(P)).then_inc(S("ld_gb1"), 16)
            sp.dma_start(g1[0:BUCKETS, 0:2 * HK], dr["bias"]).then_inc(S("ld_bias"), 16)
            ws = dr["ws"]

            for n in range(N_PRE):
                k = (n - N_PRE) % SLOTS
                if n >= SLOTS:
                    sp.wait_ge(S("used"), n - SLOTS + 1)
                cols = UNIT // 2 if n == N_WIN + N_WOUT + N_GU + N_DOWN - 1 else UNIT
                sp.dma_start(slot(k)[:, 0:cols], ws[n, :, 0:cols]).then_inc(S(f"ld_w{k}"), 16)
            def expert_units(i, e):
                for j in range(LOADS):
                    k = j % RAW
                    gone = 2 * (j - RAW) + 2 + RAW if j >= RAW else j + 1
                    sp.wait_ge(S("split"), i * HALVES + gone)
                    h = 2 * j if j < PAIRED // 2 else j + PAIRED // 2
                    at, cols = h % 2 * HALF, UNIT if h < PAIRED else HALF
                    sp.dma_start(raw[:, k * UNIT:k * UNIT + cols],
                                 ws[bass.ds(e * PER_EXPERT + (N_PRE + h // 2), 1), :, at:at + cols].rearrange("a p n -> (a p) n"),
                                 ).then_inc(S(f"ld_e{k}"), 16)

            with sp.Fori(0, EXPERTS) as i:
                expert_units(i, i)
            sp.wait_ge(S("routed"), 1)
            n_items = sp.value_load(nit[0:1, 0:1], min_val=EXPERTS, max_val=EXPERTS + 3)
            with sp.If(n_items > EXPERTS):
                with sp.Fori(EXPERTS, n_items) as i:
                    e = sp.value_load(nit[0:1, bass.ds(i - (EXPERTS - 1), 1)], min_val=0, max_val=EXPERTS - 1)
                    expert_units(i, e)
            sp.wait_ge(S("gb0_used"), 2)
            sp.dma_start(gb[:, 0:D], dr["gains"][2, :].partition_broadcast(P)).then_inc(S("ld_gb0"), 16)
            for n in range(N_POST):
                k = n % SLOTS
                if n == 0:
                    sp.wait_ge(S("split"), n_items * HALVES + RAW)
                if n == RAW:
                    sp.wait_ge(S("e_used"), n_items * HALVES + SPLIT)
                if n >= SLOTS:
                    sp.wait_ge(S("used_b"), n - SLOTS + 1)
                sp.dma_start(slot(k), ws[POST0 + n, :, :]).then_inc(S(f"ld_b{k}"), 16)
                if n == SLOTS:
                    sp.wait_ge(S("gb1_used"), 1)
                    sp.dma_start(gb[:, D:2 * D], dr["gains"][3, :].partition_broadcast(P)).then_inc(S("ld_gb1"), 16)
            for tt in range(TT):
                sp.wait_ge(S("y_ready"), tt + 1)
                sp.dma_start(out[tt * P:(tt + 1) * P, :], X[:, tt, :]).then_inc(S("stored"), 16)
            sp.wait_ge(S("stored"), 16 * TT)

        @block.gpsimd
        def _(pool):
            nc.gpsimd.memset(U[:, :, 0:TAPS - 1], 0.0).then_inc(S("pad"), 1)
            pool.wait_ge(S("ld_gb0"), 16)
            pool.wait_ge(S("h_ready"), 2)
            for tt in range(TT):
                nc.gpsimd.tensor_tensor(X[:, tt, :], X[:, tt, :], gb[:, 0:D], ALU.add).then_inc(S("gb0_used"), 1)
            pool.wait_ge(S("x_ffn"), 1)
            nc.gpsimd.memset(big[:, 0:HEADS * SEQ], 0.0).then_inc(S("pad"), 1)
            pool.wait_ge(S("att_done"), 1)
            nc.gpsimd.memset(YS, 0.0).then_inc(S("pad"), 1)
            nc.gpsimd.memset(PTX, 0.0).then_inc(S("pad"), 1)
            nc.gpsimd.memset(GS, 0.0).then_inc(S("pad"), 1)
            pool.wait_ge(S("experts_done"), 1)
            nc.gpsimd.memset(big[:, 0:GH * SEQ], 0.0).then_inc(S("pad"), 1)
            pool.wait_ge(S("hk_ready"), 1)
            pool.dma_start(dr["scratch"], f1[0:GH, 0:HK]).then_inc(S("hk_out"), 16)
            pool.wait_ge(S("hk_out"), 16)
            for h in range(GH):
                src = bass.AP(dr["scratch"].tensor, h * HK, [[1, P], [1, SEQ]])
                pool.dma_start(HKB[:, h, :], src).then_inc(S("hk_in"), 16)
            pool.wait_ge(S("att_done"), 2)
            nc.gpsimd.memset(GU_[:, :, 0:TAPS2 - 1], 0.0).then_inc(S("pad"), 1)

        def norm_act(act, B, u, ready, order, gains):
            for s, v in ready:
                act.wait_ge(s, v)
            if dbg and f"x{u}" in dbg:
                act.dma_start(dbg[f"x{u}"].rearrange("(t p) d -> p t d", p=P), X).then_inc(S("dbg"), 16)
                dbg["n"] = dbg.get("n", 0) + 16
                act.wait_ge(S("dbg"), dbg["n"])
            for tt in range(TT):
                ins = nc.scalar.activation(H[:, tt, :], X[:, tt, :], ACT.Square, accum_out=ss[:, tt:tt + 1])
                ins.then_inc(S("sumsq"), 1)
            act.wait_ge(S("meansq"), order + 1)
            nc.scalar.activation(ss[:, 4:6], ss[:, 2:4], ACT.Sqrt).then_inc(S("root"), 1)
            if gains:
                transposed(act, B, u, gains, 0)

        def transposed(eng, B, u, gains, half):
            for j in range(half, 4, 2):
                bank = filled(eng, B, ("T", u, j))
                for g, (gname, dst) in enumerate(gains):
                    for c in range(2 * j, 2 * j + 2):
                        src = bank[:, (c % 2) * SEQ:(c % 2 + 1) * SEQ]
                        if half == 0:
                            ins = nc.scalar.activation(dst[:, c, :], src, ACT.Copy, scale=V(gname, c))
                        else:
                            ins = nc.vector.tensor_scalar(dst[:, c, :], src, V(gname, c), None, ALU.mult)
                        ins.then_inc(S("ht_act" if half == 0 else "ht_dve"), 1)
                eng.wait_ge(S("ht_act" if half == 0 else "ht_dve"), ht_count[u] * 4 + (j // 2 + 1) * 2 * len(gains))
                eng.sem_inc(B.free[B.at[("T", u, j)][0]], 1)

        ht_count = {0: 0, 1: 1, 2: 2, 3: 4, 5: 5, 7: 6}

        def norm_dve(dve, ch, B, u, order, gains, normed=True):
            dve.wait_ge(S("sumsq"), 2 * (order + 1))
            nc.vector.tensor_scalar(ss[:, 2:4], ss[:, 0:2], 1.0 / D, EPS, ALU.mult, ALU.add).then_inc(S("meansq"), 1)
            dve.wait_ge(S("root"), order + 1)
            ch(nc.vector.reciprocal(ss[:, 6:8], ss[:, 4:6]))
            if normed:
                for tt in range(TT):
                    nc.vector.tensor_scalar(H[:, tt, :], X[:, tt, :], ss[:, 6 + tt:7 + tt], None, ALU.mult).then_inc(S("h_ready"), 1)
            if gains:
                transposed(dve, B, u, gains, 1)

        owed = []

        def pay(ins):
            if owed:
                ins.then_inc(S(owed.pop()), 1)
            return ins

        def norm_pe(pe, B, u, times):
            pe.wait_ge(S("h_ready"), 2 * times)
            for j in range(4):
                bank = opened(pe, B, ("T", u, j))
                for c in range(2 * j, 2 * j + 2):
                    for tt in range(TT):
                        o = (c % 2) * SEQ + tt * P
                        ins = nc.tensor.transpose(bank[:, o:o + P], H[:, tt, c * P:(c + 1) * P], C("ident"))
                        if tt == 0:
                            pay(ins)
                closed(B, ("T", u, j), ins)

        def ht_ready(pe, u, n=1):
            pe.wait_ge(S("ht_act"), 4 * (ht_count[u] + n))
            pe.wait_ge(S("ht_dve"), 4 * (ht_count[u] + n))

        def add_four(dve, B, name, done, final):
            for tt in range(TT):
                for c in range(2):
                    bank = filled(dve, B, (name, tt, c))
                    dst = X[:, tt, c * 512:(c + 1) * 512]
                    ins = nc.vector.tensor_tensor(dst, dst, bank[:, :], ALU.add)
                    s, k = let_go(B, (name, tt, c), ins)
                    dve.wait_ge(s, k)
            dve.sem_inc(S(done), 1)

        def queries_act(act, B, name, n):
            bank = filled(act, B, name)
            nc.scalar.activation(QZ[0:DH, 2 * n, :], bank[0:DH, 0:SEQ], ACT.Copy, scale=DH ** -0.5).then_inc(S("q_ready"), 1)
            ins = nc.scalar.activation(QZ[DH:P, 2 * n + 1, :], bank[DH:P, 0:SEQ], ACT.Copy, scale=DH ** -0.5)
            let_go(B, name, ins)

        def attention_act(act, B, a, heads, base):
            for h in range(heads + 2):
                if h < heads:
                    n = base + h
                    bank = filled(act, B, ("S", a, h))
                    act.wait_ge(S("rowmax"), n + 1)
                    if h >= 2:
                        b, k = B.at[("PT", a, h - 2)]
                        act.wait_ge(B.full[b], k + 1)
                    if h >= 2:
                        act.wait_ge(S("probs"), n - 1)
                    m = 8 + 4 * (h % 2)
                    nc.scalar.activation(PR[:, h % 2, 0:256], bank[:, 0:256], ACT.Exp, bias=rt[:, 64 + m:65 + m],
                                         accum_out=rt[:, 66 + m:67 + m]).then_inc(S("exps"), 1)
                    ins = nc.scalar.activation(PR[:, h % 2, 256:384], bank[:, 256:384], ACT.Exp, bias=rt[:, 65 + m:66 + m],
                                               accum_out=rt[:, 67 + m:68 + m])
                    let_go(B, ("S", a, h), ins)
                if 1 <= h <= heads:
                    bank = filled(act, B, ("PT", a, h - 1))
                    ins = nc.scalar.activation(PT[:, (h - 1) % 2, :], bank[:, 0:384], ACT.Copy)
                    let_go(B, ("PT", a, h - 1), ins)

        def half_of(t, k):
            return t[:, k * HALF:(k + 1) * HALF]

        def load_of(h):
            return h // 2 if h < PAIRED else h - PAIRED // 2

        def raw_half(h):
            return half_of(raw, load_of(h) % RAW * 2 + (h % 2 if h < PAIRED else 0))

        def high_part(act, i, h):
            if h % 2 == 0 or h >= PAIRED:
                j = load_of(h)
                act.wait_ge(S(f"ld_e{j % RAW}"), i * (16 * LOADS // RAW) + 16 * (j // RAW + 1))
            act.wait_ge(S("e_used"), i * HALVES + (h + 1))
            nc.scalar.activation(half_of(wh, h % SPLIT), raw_half(h), ACT.Copy).then_inc(S("high"), 1)

        def low_part(dve, i, h):
            dve.wait_ge(S("high"), i * HALVES + (h + 1))
            nc.vector.tensor_tensor(half_of(wl, h % SPLIT), raw_half(h), half_of(wh, h % SPLIT).bitcast(F32),
                                    ALU.subtract).then_inc(S("split"), 1)

        def item_tokens(dve, n):
            nc.vector.tensor_copy(HTGH, HTn).then_inc(S("e_hh"), 1)
            dve.wait_ge(S("e_hh"), n)
            nc.vector.tensor_tensor(HTGL, HTn, HTGH.bitcast(F32), ALU.subtract).then_inc(S("e_htg"), 1)

        def item_output(act, i):
            act.wait_ge(S("e_used"), i * HALVES + SPLIT)
            act.wait_ge(S("e_miscfree"), i * 7 + 2)
            for c in range(2):
                nc.scalar.activation(YS[:, c * 512:(c + 1) * 512], ps[4 + c][:, :], ACT.Copy,
                                     scale=GS).then_inc(S("e_ys"), 1)

        def gather_act(act, i, r):
            for half in ((0, 1) if r == 0 else (r // 2 - 1,)):
                m = half + 1 if r == 0 else i * 7 + (2 + 2 * (half + 1))
                act.wait_ge(S("e_misc"), m)
                if r:
                    act.wait_ge(S("e_htg"), i + 1)
                for c in range(4 * half, 4 * half + 4):
                    ins = nc.scalar.activation(HTn[:, c, :], ps[7][:, (c % 4) * P:(c % 4 + 1) * P], ACT.Copy,
                                               scale=V("ffn1", c))
                ins.then_inc(S("e_miscfree"), 1)

        def mix_act(act, order):
            for tt in range(TT):
                act.wait_ge(S("m_ready"), 2 * (order // 2 - 3) + tt + 1)
                nc.scalar.activation(ht_t[:, tt * D:(tt + 1) * D], M2[:, tt, :], ACT.Square,
                                     accum_out=ss[:, tt:tt + 1]).then_inc(S("sumsq"), 1)
            act.wait_ge(S("meansq"), order + 1)
            nc.scalar.activation(ss[:, 4:6], ss[:, 2:4], ACT.Sqrt).then_inc(S("root"), 1)

        def delta_act(act, ch):
            for n in range(12):
                bank = filled(act, post, ("g", n))
                if n == 0:
                    act.wait_ge(S("pad"), 7)
                ins = nc.scalar.activation(GU_[:, n, TAPS2 - 1:UP2], bank[:, 0:SEQ], ACT.Copy)
                let_go(post, ("g", n), ins)
            for tt in range(TT):
                bank = filled(act, post, ("z", tt))
                ins = nc.scalar.activation(ZS[:, tt, :], bank[:, :], ACT.Silu)
                let_go(post, ("z", tt), ins)
            for n in range(12):
                act.wait_ge(S("g_conv"), n + 1)
                nc.scalar.activation(GF[:, n, :], GF[:, n, :], ACT.Silu).then_inc(S("g_silu"), 1)
            act.wait_ge(S("ab_ready"), 1)
            ch(nc.scalar.activation(BETA, TMP[1], ACT.Exp, scale=-1.0))
            ch(nc.scalar.activation(TMP[2], TMP[0], ACT.Abs))
            ch(nc.scalar.activation(TMP[2], TMP[2], ACT.Exp, scale=-1.0))
            ch(nc.scalar.activation(TMP[2], TMP[2], ACT.Ln, bias=1.0))
            nc.scalar.activation(TMP[3][:, 0, :], row[:, R_ALOG:R_ALOG + GH], ACT.Exp).then_inc(S("ab_exp"), 1)
            act.wait_ge(S("gc_ready"), 1)
            nc.scalar.activation(EG, GC, ACT.Exp).then_inc(S("eg"), 1)
            nc.scalar.activation(EGL, TMP[4], ACT.Exp).then_inc(S("eg"), 1)
            nc.scalar.activation(GLAST, GLAST, ACT.Exp).then_inc(S("eg"), 1)
            act.wait_ge(S("l2_ready"), 1)
            nc.scalar.activation(SC2, SC2, ACT.Sqrt).then_inc(S("l2_root"), 1)
            for tt in range(TT):
                for q in range(2):
                    for n, dst in (("KT", KTt), ("QT", QTt)):
                        bank = filled(act, post, (n, tt, q))
                        ins = nc.scalar.activation(dst[:, 4 * q:4 * q + 4, :], bank[0:DH, :].rearrange("p (h s) -> p h s", s=P), ACT.Copy)
                        let_go(post, (n, tt, q), ins)
                for q in range(2):
                    bank = filled(act, post, ("DT", tt, q))
                    for h in range(4):
                        ins = nc.scalar.activation(DTs[:, q * 512 + h * P:q * 512 + (h + 1) * P], bank[:, h * P:(h + 1) * P],
                                                   ACT.Exp, bias=NGC[:, tt, 4 * q + h:4 * q + h + 1])
                        if h < 3:
                            ch.go(ins)
                    let_go(post, ("DT", tt, q), ins)
                for lv in range(LEVELS):
                    for q in range(2):
                        bank = filled(act, post, ("Z", tt, lv, q))
                        if lv == 0:
                            act.wait_ge(S("dt_used"), 2 * tt + 2)
                        ins = nc.scalar.activation(ZI[:, q * 512:(q + 1) * 512], bank[:, :], ACT.Copy)
                        let_go(post, ("Z", tt, lv, q), ins)
                for q in range(2):
                    bank = filled(act, post, ("WT", tt, q))
                    ins = nc.scalar.activation(WT[tt][:, 4 * q:4 * q + 4, :], bank[0:DH, :].rearrange("p (h s) -> p h s", s=P), ACT.Copy)
                    let_go(post, ("WT", tt, q), ins)
            for c in range(4):
                bank = filled(act, post, ("o", c))
                b0 = (c % 2) * CHUNK
                ins = nc.scalar.activation(OG[b0:b0 + CHUNK, c // 2, :], bank[b0:b0 + CHUNK, :], ACT.Copy)
                let_go(post, ("o", c), ins)
            act.wait_ge(S("o_ms"), 1)
            nc.scalar.activation(TMP[1], TMP[0], ACT.Sqrt).then_inc(S("o_root"), 1)
            for tt in range(TT):
                bank = filled(act, post, ("og", tt))
                ins = nc.scalar.activation(F3c[:, 4:8, tt * P:(tt + 1) * P], bank[:, :].rearrange("p (c s) -> p c s", s=P), ACT.Copy)
                let_go(post, ("og", tt), ins)

        @block.scalar
        def _(act):
            ch = Chain(act, "act_steps")
            act.wait_ge(S("ld_vec"), 16)
            norm_act(act, pre, 0, [(S("ld_x"), 16)], 0, [("mix0", HT)])
            act.wait_ge(S("ld_const"), 16)
            per = -(-len(DIAG) // DC)
            for i in range(DC):
                bank = filled(act, pre, ("gate", i))
                if i >= 2:
                    act.wait_ge(S("glu"), i - 1)
                ins = nc.scalar.activation(SIG[:, i % 2, :], bank[:, 0:SEQ], ACT.Sigmoid, bias=V("b_in", DC + i))
                let_go(pre, ("gate", i), ins)
                if i == 0:
                    act.wait_ge(pre.full[pre.at[("T", 0, 3)][0]], 1)
                for n in range(i * per, min((i + 1) * per, len(DIAG))):
                    w = VEC["w_dw"] + n % TAPS * DC + CONV_DVE + n // TAPS
                    nc.scalar.activation(DIAG[n], C("ident"), ACT.Copy, scale=vec[:, w:w + 1]).then_inc(S("diag"), 1)
            for i in range(CONV_DVE, DC):
                bank = filled(act, pre, ("cv", i))
                ins = nc.scalar.activation(CV[:, i, :], bank[:, 0:SEQ], ACT.Identity, bias=V("b_dw", i))
                s, k = let_go(pre, ("cv", i), ins)
                act.wait_ge(s, k)
                act.sem_inc(S("conv_pe"), 1)
            for i in range(DC):
                act.wait_ge(S("centred"), i + 1)
                nc.scalar.activation(SQ[:, i, :], CV[:, i, :], ACT.Square).then_inc(S("squares"), 1)
            bank = filled(act, pre, ("var",))
            ins = nc.scalar.activation(MUV, bank[:, 0:SEQ], ACT.Copy, scale=1.0 / D)
            s, k = let_go(pre, ("var",), ins)
            act.wait_ge(s, k)
            ch(nc.scalar.activation(MUV, MUV, ACT.Identity, bias=cst[:, EPSCOL:EPSCOL + 1]))
            nc.scalar.activation(MUV, MUV, ACT.Sqrt).then_inc(S("ln_root"), 1)
            for i in range(DC):
                act.wait_ge(S("ln_y"), i + 1)
                nc.scalar.activation(HT[:, i, :], CV[:, i, :], ACT.Silu, scale=V("ln_g", i),
                                     bias=V("ln_b", i)).then_inc(S("silu_y"), 1)
            norm_act(act, pre, 1, [(S("x_conv"), 1)], 1, [("ffn0", HT)])
            for i in range(FT):
                bank = filled(act, pre, ("ffg", i))
                if i >= 2:
                    act.wait_ge(S("ff_prod"), i - 1)
                ins = nc.scalar.activation(FFG[:, i % 2, :], bank[:, 0:SEQ], ACT.Silu)
                let_go(pre, ("ffg", i), ins)
            norm_act(act, pre, 2, [(S("x_ffn"), 1)], 2, [("mix1", HT), ("kv", F3c)])
            act.wait_ge(S("pad"), 2)
            for n in range(DC):
                queries_act(act, pre, ("q", n), n)
            bank = filled(act, pre, ("f",))
            ins = nc.scalar.activation(FA[0:HEADS, 0, :], bank[0:HEADS, 0:SEQ], ACT.Identity,
                                       bias=V("b_f", 0)[0:HEADS, :])
            s, k = let_go(pre, ("f",), ins)
            act.wait_ge(s, k)
            ch(nc.scalar.activation(FA[0:HEADS, 1, :], FA[0:HEADS, 0, :], ACT.Abs))
            ch(nc.scalar.activation(FA[0:HEADS, 1, :], FA[0:HEADS, 1, :], ACT.Exp, scale=-1.0))
            nc.scalar.activation(FA[0:HEADS, 2, :], FA[0:HEADS, 1, :], ACT.Ln, bias=1.0).then_inc(S("f_ln"), 1)
            attention_act(act, pre, 0, HEADS, 0)
            norm_act(act, pre, 3, [(S("x_att"), 1)], 3, [("ffn1", HT)])
            act.wait_ge(S("gap"), 1)
            nc.scalar.activation(rt[:, 60:62], rt[:, 58:60], ACT.Exp).then_inc(S("gap_exp"), 1)

            gather_act(act, 0, 0)
            act.wait_ge(S("routed"), 1)
            act.wait_ge(S("pad"), 5)
            n_items = act.value_load(nit[0:1, 0:1], min_val=EXPERTS, max_val=EXPERTS + 3)
            with act.Fori(0, n_items) as i:
                def silu(s):
                    w = 512 if s < 5 else 256
                    act.wait_ge(S("e_gu"), i * 12 + (2 * s + 1))
                    nc.scalar.activation(SG[:, s % 2, 0:w], ps[s % 2][:, 0:w], ACT.Silu).then_inc(S("e_silu"), 1)

                def tile_t(s):
                    w = 512 if s < 5 else 256
                    act.wait_ge(S("e_tr"), i * 6 + (s + 1))
                    nc.scalar.activation(ATEH[:, s % 2, 0:w], ps[6][:, 0:w], ACT.Copy).then_inc(S("e_ath"), 1)

                def high(*halves):
                    for h in halves:
                        high_part(act, i, h)

                nc.scalar.activation(mid[0:1, 508:509], cst[0:1, 0:1], ACT.Silu).then_inc(S("e_table"), 1)
                high(0, 1)
                item_output(act, i)
                high(2, 3, 4)
                silu(0)
                high(5, 6)
                gather_act(act, i, 2)
                high(7, 8)
                silu(1)
                tile_t(0)
                high(9, 10)
                gather_act(act, i, 4)
                high(11, 12)
                high(13, 14)
                silu(2)
                tile_t(1)
                high(15, 16, 17, 18, 19, 20)
                silu(3)
                tile_t(2)
                high(21, 22, 23, 24, 25, 26)
                act.wait_ge(S("e_misc"), i * 7 + (2 + 7))
                nc.scalar.activation(PTX, ps[7][:, 0:SEQ], ACT.Copy).then_inc(S("e_ptx"), 1)
                nc.scalar.activation(GS, ps[7][:, SEQ:SEQ + 1], ACT.Copy).then_inc(S("e_miscfree"), 1)
                silu(4)
                tile_t(3)
                high(27, 28, 29, 30)
                silu(5)
                tile_t(4)
                high(31)
                high(32)
                tile_t(5)
            item_output(act, n_items)
            norm_act(act, post, 4, [(S("experts_done"), 1)], 4, None)
            norm_act(act, post, 5, [(S("x_first"), 1)], 5, [("pre_mix", HT)])
            act.wait_ge(S("pad"), 6)
            for n in range(4):
                queries_act(act, post, ("q2", n), n)
            attention_act(act, post, 1, GH, HEADS)
            delta_act(act, ch)
            mix_act(act, 6)
            norm_act(act, post, 7, [(S("x_mix"), 1)], 7, [("pre_mlp", HT)])
            for i in range(FT2):
                bank = filled(act, post, ("up", i))
                if i >= 2:
                    act.wait_ge(S("up_prod"), i - 1)
                ins = nc.scalar.activation(FFG[:, i % 2, :], bank[:, 0:SEQ], ACT.Relu)
                let_go(post, ("up", i), ins)
            mix_act(act, 8)

        def keys_dve(dve, B, name, n):
            bank = filled(dve, B, name)
            ins = nc.vector.tensor_copy(KT[:, n, :], bank[:, 0:SEQ])
            let_go(B, name, ins)

        def attention_dve(dve, ch, B, a, heads, base):
            for h in range(heads + 2):
                if h < heads:
                    bank = filled(dve, B, ("S", a, h))
                    m = 72 + 4 * (h % 2)
                    ch.go(nc.vector.tensor_reduce(rt[:, m:m + 1], bank[:, 0:256], AX, ALU.max, negate=True))
                    ch(nc.vector.tensor_reduce(rt[:, m + 1:m + 2], bank[:, 256:384], AX, ALU.max, negate=True))
                    dve.sem_inc(S("rowmax"), 1)
                    b, k = B.at[("S", a, h)]
                    dve.wait_ge(B.free[b], k + 1)
                    dve.wait_ge(S("exps"), base + h + 1)
                    ch(nc.vector.reciprocal(rt[:, m + 16:m + 18], rt[:, m + 2:m + 4]))
                    ch.go(nc.vector.tensor_scalar(PR[:, h % 2, 0:256], PR[:, h % 2, 0:256], rt[:, m + 16:m + 17], None, ALU.mult))
                    ch(nc.vector.tensor_scalar(PR[:, h % 2, 256:384], PR[:, h % 2, 256:384], rt[:, m + 17:m + 18], None, ALU.mult))
                    dve.sem_inc(S("probs"), 1)
                if h >= 2 and h % 2 == 1:
                    bank = filled(dve, B, ("O", a, (h - 2) // 2))
                    ins = nc.vector.tensor_copy(F3c[:, (h - 2) // 2, :], bank[:, 0:SEQ])
                    s, k = let_go(B, ("O", a, (h - 2) // 2), ins)
            dve.wait_ge(s, k)
            dve.sem_inc(S("att_done"), 1)

        def route(dve, ch):
            e8 = EXPERTS

            def t3(k):
                return rt[:, 128 + 16 * k:144 + 16 * k].rearrange("p (t e) -> p t e", t=TT)

            def t2(k):
                return rt[:, 48 + 2 * k:50 + 2 * k]

            def over_experts(a):
                return a.unsqueeze(2).to_broadcast([P, TT, e8])

            def over_tiles(a):
                return a.unsqueeze(1).to_broadcast([P, TT, e8])

            iota8 = cst[:, IOTA8:IOTA8 + e8]
            LG, EQ, CAND, OH1, OH2, RT, GT, L2, PV = (t3(k) for k in range(9))
            bank = filled(dve, pre, ("logits",))
            ins = nc.vector.tensor_tensor(LG, bank[:, 0:16].rearrange("p (t e) -> p t e", t=TT),
                                          over_tiles(row[:, R_RB:R_RB + e8]), ALU.add)
            s, k = let_go(pre, ("logits",), ins)
            dve.wait_ge(s, k)

            def first_max(src, best, onehot):
                ch(nc.vector.tensor_reduce(best, src, AX, ALU.max))
                ch(nc.vector.tensor_tensor(EQ, src, over_experts(best), ALU.is_equal))
                ch(nc.vector.scalar_tensor_tensor(CAND, EQ, -float(e8), over_tiles(iota8), ALU.mult, ALU.add))
                ch(nc.vector.tensor_reduce(t2(2), CAND, AX, ALU.min))
                ch(nc.vector.tensor_tensor(onehot, CAND, over_experts(t2(2)), ALU.is_equal))

            first_max(LG, t2(0), OH1)
            ch(nc.vector.scalar_tensor_tensor(L2, OH1, -3e38, LG, ALU.mult, ALU.add))
            first_max(L2, t2(1), OH2)
            nc.vector.tensor_tensor(t2(5), t2(1), t2(0), ALU.subtract).then_inc(S("gap"), 1)
            dve.wait_ge(S("gap_exp"), 1)
            ch(nc.vector.tensor_scalar(t2(3), t2(6), 1.0, None, ALU.add))
            ch(nc.vector.reciprocal(t2(3), t2(3)))
            ch(nc.vector.tensor_tensor(t2(4), t2(3), t2(6), ALU.mult))
            ch(nc.vector.tensor_tensor(RT, OH1, OH2, ALU.add))
            dve.sem_inc(S("chosen"), 1)
            ch(nc.vector.tensor_tensor(GT, OH1, over_experts(t2(3)), ALU.mult))
            ch(nc.vector.tensor_tensor(EQ, OH2, over_experts(t2(4)), ALU.mult))
            ch(nc.vector.tensor_tensor(GT, GT, EQ, ALU.add))
            bank = filled(dve, pre, ("pos",))
            ch(nc.vector.scalar_tensor_tensor(PV, bank[:, 0:16].rearrange("p (t e) -> p t e", t=TT), 1.0, RT,
                                              ALU.add, ALU.mult))
            cnt, over, rank, sel = (rt[:, 288 + 8 * k:296 + 8 * k] for k in range(4))
            ins = nc.vector.tensor_copy(cnt, bank[:, 16:24])
            s, k = let_go(pre, ("pos",), ins)
            dve.wait_ge(s, k)
            ch(nc.vector.memset(POSI, -1000.0))
            ch(nc.vector.memset(GATI, 0.0))
            ch(nc.vector.tensor_scalar(POSI[:, :, 0:e8], PV, -1.0, None, ALU.add))
            ch(nc.vector.tensor_copy(GATI[:, :, 0:e8], GT))
            ch(nc.vector.tensor_scalar(over, cnt, float(P), None, ALU.is_gt))
            ch(nc.vector.memset(rt[:, 320:328], 1.0))
            ch(nc.vector.tensor_tensor_scan(rank, rt[:, 320:328], over, 0.0, ALU.mult, ALU.add))
            meta = rt[:, 328:332]
            ch(nc.vector.tensor_scalar(meta[:, 0:1], rank[:, 7:8], float(e8), None, ALU.add))
            for k in range(3):
                ch(nc.vector.scalar_tensor_tensor(sel, rank, float(k + 1), over, ALU.is_equal, ALU.mult))
                ch(nc.vector.tensor_tensor(EQ, PV, over_tiles(sel), ALU.mult))
                ch(nc.vector.tensor_reduce(t2(2), EQ, AX, ALU.add))
                ch(nc.vector.tensor_scalar(POSI[:, :, e8 + k], t2(2), -(1.0 + P), None, ALU.add))
                ch(nc.vector.tensor_tensor(EQ, GT, over_tiles(sel), ALU.mult))
                ch(nc.vector.tensor_reduce(t2(2), EQ, AX, ALU.add))
                ch(nc.vector.tensor_copy(GATI[:, :, e8 + k], t2(2)))
                ch(nc.vector.tensor_tensor(rt[:, 336:344], sel, iota8, ALU.mult))
                ch(nc.vector.tensor_reduce(meta[:, k + 1:k + 2], rt[:, 336:344], AX, ALU.add))
            ch(nc.vector.tensor_copy(nit[:, 0:4], meta))
            dve.sem_inc(S("routed"), 1)

        def select(dve, dst, i, ahead, done, gate_of):
            if gate_of is None:
                cols = POSI[:, :, 0]
            else:
                base = gate_of[1]
                at = i + ahead
                nc.vector.tensor_copy(CP[:, base:base + 2].unsqueeze(2), POSI[:, :, bass.ds(at, 1)]).then_inc(S("e_cp"), 1)
                if ahead == 0:
                    nc.vector.tensor_copy(rt[:, 400:402].unsqueeze(2), GATI[:, :, bass.ds(at, 1)]).then_inc(S("e_cp"), 1)
                dve.wait_ge(S("e_cp"), i * 3 + (1 if ahead else 3))
                cols = CP[:, base:base + 2]
            for tt in range(TT):
                nc.vector.tensor_scalar(dst[:, tt, :], C("iota"), cols[:, tt:tt + 1], None,
                                        ALU.is_equal).then_inc(S(done), 1)

        def mix_dve(dve, ch, name, order, gbn, done):
            for tt in range(TT):
                for c in range(2):
                    bank = filled(dve, post, (name, tt, c))
                    ins = nc.vector.tensor_copy(M2[:, tt, c * 512:(c + 1) * 512], bank[:, :])
                    s, k = let_go(post, (name, tt, c), ins)
                    dve.wait_ge(s, k)
                dve.sem_inc(S("m_ready"), 1)
            dve.wait_ge(S("sumsq"), 2 * (order + 1))
            nc.vector.tensor_scalar(ss[:, 2:4], ss[:, 0:2], 1.0 / D, EPS, ALU.mult, ALU.add).then_inc(S("meansq"), 1)
            dve.wait_ge(S("root"), order + 1)
            ch(nc.vector.reciprocal(ss[:, 6:8], ss[:, 4:6]))
            dve.wait_ge(S(f"ld_gb{gbn}"), 32)
            for tt in range(TT):
                ch(nc.vector.scalar_tensor_tensor(M2[:, tt, :], M2[:, tt, :], ss[:, 6 + tt:7 + tt],
                                                  gb[:, gbn * D:(gbn + 1) * D], ALU.mult, ALU.mult))
                ch(nc.vector.tensor_tensor(X[:, tt, :], X[:, tt, :], M2[:, tt, :], ALU.add))
                if done == "y_ready":
                    dve.sem_inc(S(done), 1)
            if done != "y_ready":
                dve.sem_inc(S(done), 1)

        def heads(a):
            return a.rearrange("p t (h d) -> p t h d", d=DH)

        def per_head(a, tt=None):
            if tt is None:
                return a.unsqueeze(3).to_broadcast([P, TT, GH, DH])
            return a[:, tt, :].unsqueeze(2).to_broadcast([P, GH, DH])

        def delta_dve(dve, ch):
            for n in range(12):
                b, k = post.at[("g", n)]
                dve.wait_ge(post.free[b], k + 1)
                for t in range(TAPS2):
                    w = vec[:, VEC["conv2"] + t * 12 + n:VEC["conv2"] + t * 12 + n + 1]
                    src = GU_[:, n, t:t + SEQ]
                    if t == 0:
                        ins = nc.vector.tensor_scalar(GF[:, n, :], src, w, None, ALU.mult)
                    else:
                        ins = nc.vector.scalar_tensor_tensor(GF[:, n, :], src, w, GF[:, n, :], ALU.mult, ALU.add)
                    if t < TAPS2 - 1:
                        ch(ins)
                ins.then_inc(S("g_conv"), 1)
            bank = filled(dve, post, ("ab",))
            v = bank[:, 0:32].rearrange("p (t n) -> p t n", t=TT)
            ch(nc.vector.tensor_tensor(TMP[0], v[:, :, 0:GH], row[:, R_DT:R_DT + GH].unsqueeze(1).to_broadcast([P, TT, GH]), ALU.add))
            ins = nc.vector.tensor_copy(TMP[1], v[:, :, GH:2 * GH])
            s, k = let_go(post, ("ab",), ins)
            dve.wait_ge(s, k)
            dve.sem_inc(S("ab_ready"), 1)
            dve.wait_ge(S("ab_exp"), 1)
            ch(nc.vector.tensor_scalar(BETA, BETA, 1.0, None, ALU.add))
            ch(nc.vector.reciprocal(BETA, BETA))
            ch(nc.vector.scalar_tensor_tensor(TMP[2], TMP[0], 0.0, TMP[2], ALU.max, ALU.add))
            ch(nc.vector.scalar_tensor_tensor(GLOG, TMP[2], -1.0, TMP[3][:, 0, :].unsqueeze(1).to_broadcast([P, TT, GH]),
                                              ALU.mult, ALU.mult))
            dve.sem_inc(S("glog"), 1)
            bank = filled(dve, post, ("gcum",))
            v = bank[:, 0:32].rearrange("p (j t n) -> p j t n", j=2, t=TT)
            ch(nc.vector.tensor_copy(GC, v[:, 0]))
            dve.sem_inc(S("gcum_ready"), 1)
            ch(nc.vector.tensor_scalar(NGC, GC, -1.0, None, ALU.mult))
            ch(nc.vector.tensor_tensor(TMP[4], v[:, 1], GC, ALU.subtract))
            bank2 = filled(dve, post, ("gT",))
            ch(nc.vector.tensor_copy(GTR, bank2[0:GH, 0:SEQ]))
            ins = nc.vector.tensor_copy(GLAST, bank2[:, SEQ:SEQ + 32].rearrange("p (c h) -> p c h", c=4))
            s, k = let_go(post, ("gT",), ins)
            dve.wait_ge(s, k)
            dve.sem_inc(post.free[post.at[("gcum",)][0]], 1)
            dve.sem_inc(S("gc_ready"), 1)
            for tt in range(TT):
                for j in range(3):
                    bank = filled(dve, post, ("tm", tt, j))
                    ins = nc.vector.tensor_copy(TM[:, tt, j, :], bank[:, :])
                    s, k = let_go(post, ("tm", tt, j), ins)
                    dve.wait_ge(s, k)
            for j in range(2):
                ch(nc.vector.tensor_tensor(RW, TM[:, :, j, :], TM[:, :, j, :], ALU.mult))
                ch(nc.vector.tensor_reduce(SC2[:, j], heads(RW), AX, ALU.add))
            ch(nc.vector.tensor_scalar(SC2, SC2, EPS, None, ALU.add))
            dve.sem_inc(S("l2_ready"), 1)
            dve.wait_ge(S("l2_root"), 1)
            ch(nc.vector.reciprocal(SC2, SC2))
            ch(nc.vector.tensor_scalar(SC2[:, 0], SC2[:, 0], DH ** -0.5, None, ALU.mult))
            dve.wait_ge(S("eg"), 3)
            for tt in range(TT):
                q3, k3, v3 = (TM[:, tt, j, :].rearrange("p (h d) -> p h d", d=DH) for j in range(3))

                def hd(a):
                    return a[:, tt, :].rearrange("p (h d) -> p h d", d=DH)

                def mul(o, a, s):
                    ch(nc.vector.tensor_tensor(o, a, s.unsqueeze(2).to_broadcast([P, GH, DH]), ALU.mult))

                qn, kn = (a.rearrange("p (h d) -> p h d", d=DH) for a in (QN[tt], KN[tt]))
                mul(qn, q3, SC2[:, 0, tt, :])
                mul(kn, k3, SC2[:, 1, tt, :])
                q3, k3 = qn, kn
                mul(hd(KB), k3, BETA[:, tt, :])
                mul(hd(QD), q3, EG[:, tt, :])
                mul(hd(RW), hd(KB), EG[:, tt, :])
                mul(hd(KD), k3, EGL[:, tt, :])
                mul(hd(VB), v3, BETA[:, tt, :])
                dve.sem_inc(S("tm_ready"), 1)
            for tt in range(TT):
                for q in range(2):
                    for n, dst in (("KBT", KBTt), ("QDT", QDT)):
                        bank = filled(dve, post, (n, tt, q))
                        src = bank[0:DH, :].rearrange("p (h s) -> p h s", s=P)
                        d = dst[:, 4 * q:4 * q + 4, :] if n == "KBT" else dst[:, 4 * q:4 * q + 4, tt * P:(tt + 1) * P]
                        ins = nc.vector.tensor_copy(d, src)
                        let_go(post, (n, tt, q), ins)
                for q in range(2):
                    b, k = post.at[("DT", tt, q)]
                    dve.wait_ge(post.free[b], k + 1)
                    bank = filled(dve, post, ("KK", tt, q))
                    dt = DTs[:, q * 512:(q + 1) * 512]
                    ins = nc.vector.tensor_tensor(MTv(tt)[:, q * 512:(q + 1) * 512], bank[:, :], dt, ALU.mult)
                    s, k = let_go(post, ("KK", tt, q), ins)
                    dve.wait_ge(s, k)
                    bank = filled(dve, post, ("QK", tt, q))
                    ins = nc.vector.tensor_tensor(ATG[:, tt, 4 * q:4 * q + 4, :], bank[:, :].rearrange("p (h s) -> p h s", s=P),
                                                  dt.rearrange("p (h s) -> p h s", s=P), ALU.mult)
                    s, k = let_go(post, ("QK", tt, q), ins)
                    dve.wait_ge(s, k)
                    dve.sem_inc(S("dt_used"), 1)
                idb = C("ident").unsqueeze(1).to_broadcast([P, GH, P])
                ch.go(nc.vector.tensor_copy(XI.rearrange("p (h s) -> p h s", s=P), idb))
                ch(nc.vector.tensor_copy(WI.rearrange("p (h s) -> p h s", s=P), idb))
                for lv in range(LEVELS):
                    m = cst[:, LEVEL0 + lv * P:LEVEL0 + (lv + 1) * P].unsqueeze(1).to_broadcast([P, GH, P])
                    if lv:
                        b, k = post.at[("Z", tt, lv - 1, 1)]
                        dve.wait_ge(post.full[b], k + 1)
                    ch(nc.vector.tensor_tensor(CI.rearrange("p (h s) -> p h s", s=P), MTv(tt).rearrange("p (h s) -> p h s", s=P), m, ALU.mult))
                    dve.sem_inc(S("ci_ready"), 1)
                    for q in range(2):
                        for n, dst in (("XZ", XI), ("ZW", WI)):
                            if n == "XZ":
                                b, k = post.at[("ZW", tt, lv, q)]
                                dve.wait_ge(post.full[b], k + 1)
                            bank = filled(dve, post, (n, tt, lv, q))
                            d = dst[:, q * 512:(q + 1) * 512]
                            ins = nc.vector.tensor_tensor(d, d, bank[:, :], ALU.subtract)
                            s, k = let_go(post, (n, tt, lv, q), ins)
                            dve.wait_ge(s, k)
                    dve.sem_inc(S("level"), 1)
                bank = filled(dve, post, ("U", tt))
                ins = nc.vector.tensor_copy(UU[:, tt, :], bank[:, :])
                let_go(post, ("U", tt), ins)
            b, k = post.at[("WT", 1, 1)]
            dve.wait_ge(post.full[b], k + 1)
            ch.go(nc.vector.memset(VN[0], 0.0))
            ch.go(nc.vector.memset(VN[1], 0.0))
            ch(nc.vector.memset(ST, 0.0))
            dve.sem_inc(S("st_ready"), 1)
            for c in range(4):
                tt, b0 = c // 2, (c % 2) * CHUNK
                bank = filled(dve, post, ("vn", c))
                if c >= 2:
                    b, k = post.at[("st", c - 2)]
                    dve.wait_ge(post.full[b], k + 1)
                ins = nc.vector.tensor_tensor(VN[c % 2][b0:b0 + CHUNK, :], UU[b0:b0 + CHUNK, tt, :], bank[b0:b0 + CHUNK, :], ALU.subtract)
                s, k = let_go(post, ("vn", c), ins)
                dve.wait_ge(s, k)
                dve.sem_inc(S("vn_ready"), 1)
                gl = GLAST[0:DH, c, :].unsqueeze(2).to_broadcast([DH, GH, DH])
                ch(nc.vector.tensor_tensor(STT_, ST, gl, ALU.mult))
                bank = filled(dve, post, ("st", c))
                ins = nc.vector.tensor_tensor(ST, STT_, bank[0:DH, :].rearrange("p (h v) -> p h v", v=DH), ALU.add)
                s, k = let_go(post, ("st", c), ins)
                dve.wait_ge(s, k)
                dve.sem_inc(S("st_ready"), 1)
            b, k = post.at[("o", 3)]
            dve.wait_ge(post.free[b], k + 1)
            b, k = post.at[("o", 2)]
            dve.wait_ge(post.free[b], k + 1)
            b, k = post.at[("o", 1)]
            dve.wait_ge(post.free[b], k + 1)
            b, k = post.at[("o", 0)]
            dve.wait_ge(post.free[b], k + 1)
            ch(nc.vector.tensor_tensor(OSQ, OG, OG, ALU.mult))
            ch(nc.vector.tensor_reduce(TMP[0], heads(OSQ), AX, ALU.add))
            ch(nc.vector.tensor_scalar(TMP[0], TMP[0], 1.0 / DH, EPS, ALU.mult, ALU.add))
            dve.sem_inc(S("o_ms"), 1)
            dve.wait_ge(S("o_root"), 1)
            ch(nc.vector.reciprocal(TMP[2], TMP[1]))
            for tt in range(TT):
                o3 = OG[:, tt, :].rearrange("p (h d) -> p h d", d=DH)
                ch(nc.vector.tensor_tensor(o3, o3, per_head(TMP[2], tt), ALU.mult))
                ch(nc.vector.tensor_tensor(o3, o3, row[:, R_NORM:R_NORM + DH].unsqueeze(1).to_broadcast([P, GH, DH]), ALU.mult))
                ch(nc.vector.tensor_tensor(OG[:, tt, :], OG[:, tt, :], ZS[:, tt, :], ALU.mult))
                dve.sem_inc(S("og_ready"), 1)

        def MTv(tt):
            return MT

        @block.vector
        def _(dve):
            ch = Chain(dve, "dve_steps")
            dve.wait_ge(S("ld_const"), 16)
            dve.wait_ge(S("ld_row"), 16)
            dve.wait_ge(S("ld_vec"), 16)
            norm_dve(dve, ch, pre, 0, 0, [("mix0", HT)])
            dve.wait_ge(S("pad"), 1)
            def glu(i):
                bank = filled(dve, pre, ("a", i))
                b, k = pre.at[("gate", i)]
                dve.wait_ge(pre.free[b], k + 1)
                ins = nc.vector.scalar_tensor_tensor(U[:, i, TAPS - 1:UPAD], bank[:, 0:SEQ], V("b_in", i),
                                                     SIG[:, i % 2, :], ALU.add, ALU.mult)
                s, k = let_go(pre, ("a", i), ins)
                dve.wait_ge(s, k)
                dve.sem_inc(S("glu"), 1)

            def taps(i):
                for t in range(TAPS):
                    acc = (CV, CVB)[t % 2][:, i, :]
                    src, w = U[:, i, t:t + SEQ], vec[:, VEC["w_dw"] + t * DC + i:VEC["w_dw"] + t * DC + i + 1]
                    if t >= 2:
                        ch.join(1)
                    if t == 0:
                        ch.go(nc.vector.tensor_scalar(acc, src, w, V("b_dw", i), ALU.mult, ALU.add))
                    elif t == 1:
                        ch.go(nc.vector.tensor_scalar(acc, src, w, None, ALU.mult))
                    else:
                        ch.go(nc.vector.scalar_tensor_tensor(acc, src, w, acc, ALU.mult, ALU.add))
                ch.join()
                nc.vector.tensor_tensor(CV[:, i, :], CV[:, i, :], CVB[:, i, :], ALU.add).then_inc(S("conv"), 1)

            for i in range(4):
                glu(i)
                taps(i)
            glu(4)
            glu(5)
            glu(6)
            taps(4)
            glu(7)
            taps(5)
            dve.wait_ge(S("conv"), CONV_DVE)
            dve.wait_ge(S("conv_pe"), DC - CONV_DVE)
            bank = filled(dve, pre, ("mu",))
            for i in range(DC):
                nc.vector.scalar_tensor_tensor(CV[:, i, :], bank[:, 0:SEQ], -1.0 / D, CV[:, i, :], ALU.mult,
                                               ALU.add).then_inc(S("centred"), 1)
            dve.wait_ge(S("centred"), DC)
            dve.sem_inc(pre.free[pre.at[("mu",)][0]], 1)
            dve.wait_ge(S("ln_root"), 1)
            ch(nc.vector.reciprocal(MUV, MUV))
            for i in range(DC):
                nc.vector.tensor_tensor(CV[:, i, :], CV[:, i, :], MUV, ALU.mult).then_inc(S("ln_y"), 1)
            dve.wait_ge(S("gb0_used"), 2)
            add_four(dve, pre, "wout", "x_conv", None)
            norm_dve(dve, ch, pre, 1, 1, [("ffn0", HT)])
            for i in range(FT):
                bank = filled(dve, pre, ("ffu", i))
                b, k = pre.at[("ffg", i)]
                dve.wait_ge(pre.free[b], k + 1)
                ins = nc.vector.tensor_tensor(AT[:, i, :], bank[:, 0:SEQ], FFG[:, i % 2, :], ALU.mult)
                s, k = let_go(pre, ("ffu", i), ins)
                dve.wait_ge(s, k)
                dve.sem_inc(S("ff_prod"), 1)
            add_four(dve, pre, "ffd", "x_ffn", None)
            norm_dve(dve, ch, pre, 2, 2, [("mix1", HT), ("kv", F3c)])
            for n in range(DC):
                keys_dve(dve, pre, ("k", n), n)
            for tt in range(TT):
                for c in range(2):
                    bank = filled(dve, pre, ("v", tt, c))
                    ins = nc.vector.tensor_copy(f2[:, tt * D + c * 512:tt * D + (c + 1) * 512], bank[:, :])
                    let_go(pre, ("v", tt, c), ins)
            dve.sem_inc(S("split"), RAW)
            dve.wait_ge(S("f_ln"), 1)
            ch(nc.vector.memset(FA[0:HEADS, 3, :], 1.0))
            ch(nc.vector.memset(NL, 0.0))
            ch(nc.vector.scalar_tensor_tensor(FA[0:HEADS, 1, :], FA[0:HEADS, 0, :], 0.0, FA[0:HEADS, 2, :],
                                              ALU.min, ALU.subtract))
            nc.vector.tensor_tensor_scan(NL[0:HEADS, :], FA[0:HEADS, 3, :], FA[0:HEADS, 1, :], 0.0, ALU.mult,
                                         ALU.subtract).then_inc(S("nl_ready"), 1)
            attention_dve(dve, ch, pre, 0, HEADS, 0)
            add_four(dve, pre, "wo", "x_att", None)
            norm_dve(dve, ch, pre, 3, 3, [("ffn1", HT)])
            route(dve, ch)
            select(dve, PG, 0, 0, "e_pg", None)
            dve.wait_ge(S("e_miscfree"), 2)
            item_tokens(dve, 1)
            n_items = dve.value_load(nit[0:1, 0:1], min_val=EXPERTS, max_val=EXPERTS + 3)
            with dve.Fori(0, n_items) as i:
                def scatter(r):
                    tt, c = r // 2, r % 2
                    dve.wait_ge(S("e_misc"), i * 7 + (2 + (1, 3, 5, 6)[r]))
                    dst = X[:, tt, c * 512:(c + 1) * 512]
                    nc.vector.tensor_tensor(dst, dst, ps[7][:, :], ALU.add).then_inc(S("e_miscfree"), 1)

                def product(s):
                    w = 512 if s < 5 else 256
                    dve.wait_ge(S("e_gu"), i * 12 + (2 * s + 2))
                    dve.wait_ge(S("e_silu"), i * 6 + (s + 1))
                    nc.vector.tensor_tensor(PRD[:, s % 2, 0:w], ps[2 + s % 2][:, 0:w], SG[:, s % 2, 0:w],
                                            ALU.mult).then_inc(S("e_prod"), 1)

                def low(*halves):
                    for h in halves:
                        low_part(dve, i, h)

                def tile_low(s):
                    w = 512 if s < 5 else 256
                    dve.wait_ge(S("e_ath"), i * 6 + (s + 1))
                    nc.vector.tensor_tensor(ATEL[:, s % 2, 0:w], ps[6][:, 0:w], ATEH[:, s % 2, 0:w].bitcast(F32),
                                            ALU.subtract).then_inc(S("e_at"), 1)

                low(0, 1)
                select(dve, PG, i, 1, "e_pg", (i, 0))
                low(2, 3, 4)
                scatter(0)
                low(5, 6)
                product(0)
                select(dve, PX, i, 0, "e_px", (i, 2))
                low(7, 8)
                scatter(1)
                tile_low(0)
                low(9, 10)
                product(1)
                low(11, 12, 13, 14)
                scatter(2)
                tile_low(1)
                low(15, 16)
                product(2)
                low(17, 18, 19, 20)
                scatter(3)
                tile_low(2)
                low(21, 22)
                product(3)
                low(23, 24, 25, 26)
                tile_low(3)
                low(27, 28)
                product(4)
                low(29, 30)
                tile_low(4)
                low(31)
                product(5)
                low(32)
                tile_low(5)
                dve.wait_ge(S("e_miscfree"), i * 7 + (2 + 7))
                item_tokens(dve, i + 2)
            for r in range(4):
                tt, c = r // 2, r % 2
                dve.wait_ge(S("last_full"), r + 1)
                dst = X[:, tt, c * 512:(c + 1) * 512]
                nc.vector.tensor_tensor(dst, dst, ps[4 + r][:, :], ALU.add).then_inc(S("last_added"), 1)
            dve.wait_ge(S("last_added"), 4)
            dve.sem_inc(S("experts_done"), 1)
            norm_dve(dve, ch, post, 4, 4, None, normed=False)
            dve.wait_ge(S("ld_gb1"), 16)
            for tt in range(TT):
                ch(nc.vector.scalar_tensor_tensor(X[:, tt, :], X[:, tt, :], ss[:, 6 + tt:7 + tt], gb[:, D:2 * D],
                                                  ALU.mult, ALU.mult))
            dve.sem_inc(S("x_first"), 1)
            dve.sem_inc(S("gb1_used"), 1)
            bank = filled(dve, post, ("hk",))
            ins = nc.vector.tensor_tensor(f1[0:GH, 0:HK], bank[0:GH, 0:HK], g1[0:GH, HK:2 * HK], ALU.add)
            s, k = let_go(post, ("hk",), ins)
            dve.wait_ge(s, k)
            dve.sem_inc(S("hk_ready"), 1)
            norm_dve(dve, ch, post, 5, 5, [("pre_mix", HT)])
            dve.wait_ge(S("hk_out"), 16)
            for n in range(4):
                keys_dve(dve, post, ("k2", n), n)
            for tt in range(TT):
                bank = filled(dve, post, ("v2", tt))
                ins = nc.vector.tensor_copy(f2[:, tt * 512:(tt + 1) * 512], bank[:, :])
                let_go(post, ("v2", tt), ins)
            attention_dve(dve, ch, post, 1, GH, HEADS)
            delta_dve(dve, ch)
            mix_dve(dve, ch, "mix", 6, 0, "x_mix")
            norm_dve(dve, ch, post, 7, 7, [("pre_mlp", HT)])
            for i in range(FT2):
                b, k = post.at[("up", i)]
                dve.wait_ge(post.free[b], k + 1)
                nc.vector.tensor_tensor(AT[:, i, :], FFG[:, i % 2, :], FFG[:, i % 2, :], ALU.mult).then_inc(S("up_prod"), 1)
            mix_dve(dve, ch, "mlp", 8, 1, "y_ready")

        @block.tensor
        def _(pe):
            ident = C("ident")
            count = {"n": 0}

            def unit(n_phase=None):
                n = count["n"]
                count["n"] += 1
                if n < N_PRE:
                    k = (n - N_PRE) % SLOTS
                    times = sum(1 for m in range(n + 1) if (m - N_PRE) % SLOTS == k)
                    pe.wait_ge(S(f"ld_w{k}"), 16 * times)
                else:
                    n -= N_PRE
                    k = n % SLOTS
                    pe.wait_ge(S(f"ld_b{k}"), 16 * (n // SLOTS + 1))
                return slot(k)

            def used():
                assert not owed
                owed.append("used" if count["n"] <= N_PRE else "used_b")

            def feature_tile(B, name, w, src, m=P):
                bank = opened(pe, B, name)
                for c in range(DC):
                    ins = nc.tensor.matmul(bank[0:m, 0:SEQ], w(c), src[:, c, :], start=(c == 0), stop=(c == DC - 1))
                    if c == 0:
                        pay(ins)
                closed(B, name, ins)
                return ins

            def token_tiles(B, name, src, halves=2, last=None):
                for c in range(halves):
                    w = unit().rearrange("p (c n) -> p c n", c=DC)
                    for tt in range(TT):
                        key = (name, tt, c) if halves == 2 else (name, tt)
                        bank = opened(pe, B, key)
                        for k in range(DC):
                            ins = nc.tensor.matmul(bank[:, :], src[:, k, tt * P:(tt + 1) * P], w[:, k, :],
                                                   start=(k == 0), stop=(k == DC - 1))
                            if k == 0:
                                pay(ins)
                        closed(B, key, ins)
                    used()

            def down(B, name, src, tiles):
                banks = {}
                for f in range(tiles):
                    if f % 4 == 0:
                        w = unit().rearrange("p (f n) -> p f n", f=4)
                    for tt in range(TT):
                        for c in range(2):
                            if f == 0:
                                banks[tt, c] = opened(pe, B, (name, tt, c))
                            ins = nc.tensor.matmul(banks[tt, c][:, :], src[:, f, tt * P:(tt + 1) * P],
                                                   w[:, f % 4, c * 512:(c + 1) * 512], start=(f == 0), stop=(f == tiles - 1))
                            if f == tiles - 1:
                                ins.then_inc(B.full[B.at[(name, tt, c)][0]], 1)
                            else:
                                pay(ins)
                    if f % 4 == 3 or f == tiles - 1:
                        used()

            def attention_pe(B, a, heads):
                qs = QZ
                for h in range(heads + 2):
                    if h < heads:
                        bank = opened(pe, B, ("S", a, h))
                        for lo, hi, q0 in ((0, 256, P), (256, 384, 0)):
                            nk = hi - lo
                            nc.tensor.matmul(bank[:, lo:hi], qs[:, h, q0:q0 + P], KT[:, h // 2, 0:nk], start=True, stop=False)
                            if a == 0:
                                nc.tensor.matmul(bank[:, lo:hi], ident[:, h:h + 1].to_broadcast([P, P]), NL[:, 0:nk],
                                                 start=False, stop=False)
                                ins = nc.tensor.matmul(bank[:, hi - P:hi], ident, C("causal"), start=False, stop=True)
                            else:
                                ins = nc.tensor.matmul(bank[:, lo:hi], C("anti"), HKB[:, h, SEQ - nk:SEQ],
                                                       start=False, stop=True)
                        closed(B, ("S", a, h), ins)
                    if 1 <= h <= heads:
                        g = h - 1
                        pe.wait_ge(S("probs"), (0 if a == 0 else HEADS) + g + 1)
                        bank = opened(pe, B, ("PT", a, g))
                        for j in range(3):
                            ins = nc.tensor.transpose(bank[:, j * P:(j + 1) * P], PR[:, g % 2, j * P:(j + 1) * P], ident)
                        closed(B, ("PT", a, g), ins)
                    if h >= 2:
                        g = h - 2
                        b, k = B.at[("PT", a, g)]
                        pe.wait_ge(B.free[b], k + 1)
                        name = ("O", a, g // 2)
                        bank = opened(pe, B, name) if g % 2 == 0 else ps[B.at[name][0]]
                        r = (g % 2) * DH
                        vw = D if a == 0 else 512
                        v = [f2[:, t * vw + g * DH:t * vw + (g + 1) * DH] for t in range(TT)]
                        nc.tensor.matmul(bank[r:r + DH, 0:P], v[0], PT[:, g % 2, 256:384], start=True, stop=True)
                        nc.tensor.matmul(bank[r:r + DH, P:SEQ], v[0], PT[:, g % 2, 0:P], start=True, stop=False)
                        ins = nc.tensor.matmul(bank[r:r + DH, P:SEQ], v[1], PT[:, g % 2, P:256], start=False, stop=True)
                        if g % 2:
                            closed(B, name, ins)

            pe.wait_ge(S("ld_const"), 16)
            pe.wait_ge(S("ld_vec"), 16)
            norm_pe(pe, pre, 0, 1)
            ht_ready(pe, 0)
            for u in range(N_WIN):
                w = unit().rearrange("p (c n) -> p c n", c=DC)
                for i in range(2):
                    for name, o in (("gate", 256), ("a", 0)):
                        ins = feature_tile(pre, (name, 2 * u + i), lambda c, o=o, i=i: w[:, c, o + i * P:o + (i + 1) * P], HT)
                used()
            pe.wait_ge(S("pad"), 1)
            for i in range(CONV_DVE, DC):
                bank = opened(pe, pre, ("cv", i))
                pe.wait_ge(S("glu"), i + 1)
                pe.wait_ge(S("diag"), (i - CONV_DVE + 1) * TAPS)
                for t in range(TAPS):
                    ins = nc.tensor.matmul(bank[:, 0:SEQ], DIAG[(i - CONV_DVE) * TAPS + t], U[:, i, t:t + SEQ],
                                           start=(t == 0), stop=(t == TAPS - 1))
                    if t == 0:
                        pay(ins)
                closed(pre, ("cv", i), ins)
            bank = opened(pe, pre, ("mu",))
            for c in range(DC):
                if c < CONV_DVE:
                    pe.wait_ge(S("conv"), c + 1)
                else:
                    pe.wait_ge(S("conv_pe"), c - CONV_DVE + 1)
                ins = nc.tensor.matmul(bank[:, 0:SEQ], C("ones"), CV[:, c, :], start=(c == 0), stop=(c == DC - 1))
            closed(pre, ("mu",), ins)
            bank = opened(pe, pre, ("var",))
            for c in range(DC):
                pe.wait_ge(S("squares"), c + 1)
                ins = nc.tensor.matmul(bank[:, 0:SEQ], C("ones"), SQ[:, c, :], start=(c == 0), stop=(c == DC - 1))
            closed(pre, ("var",), ins)
            pe.wait_ge(S("silu_y"), DC)
            token_tiles(pre, "wout", HT)
            norm_pe(pe, pre, 1, 2)
            ht_ready(pe, 1)
            for u in range(N_GU):
                w = unit().rearrange("p (c n) -> p c n", c=DC)
                for i in range(2):
                    for name, o in (("ffg", 0), ("ffu", 256)):
                        ins = feature_tile(pre, (name, 2 * u + i), lambda c, o=o, i=i: w[:, c, o + i * P:o + (i + 1) * P], HT)
                used()
            pe.wait_ge(S("ff_prod"), FT)
            down(pre, "ffd", AT, FT)
            norm_pe(pe, pre, 2, 3)
            ht_ready(pe, 2, 2)
            for name, src in (("q", HT), ("k", F3c)):
                for u in range(2):
                    w = unit().rearrange("p (c n) -> p c n", c=DC)
                    for i in range(4):
                        ins = feature_tile(pre, (name, 4 * u + i), lambda c, i=i: w[:, c, i * P:(i + 1) * P], src)
                    used()
            token_tiles(pre, "v", F3c)
            wf = nar[:, WF:WF + DC * HEADS].rearrange("p (c n) -> p c n", c=DC)
            pe.wait_ge(S("ld_narrow"), 16)
            feature_tile(pre, ("f",), lambda c: wf[:, c, :], F3c, m=HEADS)
            pe.wait_ge(S("q_ready"), DC)
            b, k = pre.at[("q", DC - 1)]
            pe.wait_ge(pre.free[b], k + 1)
            b, k = pre.at[("v", 1, 1)]
            pe.wait_ge(pre.free[b], k + 1)
            pe.wait_ge(S("nl_ready"), 1)
            attention_pe(pre, 0, HEADS)
            pe.wait_ge(S("att_done"), 1)
            token_tiles(pre, "wo", F3c)
            norm_pe(pe, pre, 3, 4)
            ht_ready(pe, 3)
            wr = nar[:, WR:WR + DC * EXPERTS].rearrange("p (c n) -> p c n", c=DC)
            bank = opened(pe, pre, ("logits",))
            for tt in range(TT):
                for c in range(DC):
                    ins = nc.tensor.matmul(bank[:, tt * EXPERTS:(tt + 1) * EXPERTS], HT[:, c, tt * P:(tt + 1) * P], wr[:, c, :],
                                           start=(c == 0), stop=(c == DC - 1))
            closed(pre, ("logits",), ins)
            pe.wait_ge(S("chosen"), 1)
            bank = opened(pe, pre, ("pos",))
            RT = rt[:, 128 + 80:144 + 80].rearrange("p (t e) -> p t e", t=TT)
            e8 = EXPERTS
            nc.tensor.matmul(bank[:, 0:e8], C("before"), RT[:, 0, :], start=True, stop=True)
            nc.tensor.matmul(bank[:, e8:2 * e8], C("ones"), RT[:, 0, :], start=True, stop=False)
            nc.tensor.matmul(bank[:, e8:2 * e8], C("before"), RT[:, 1, :], start=False, stop=True)
            nc.tensor.matmul(bank[:, 2 * e8:3 * e8], C("ones"), RT[:, 0, :], start=True, stop=False)
            ins = nc.tensor.matmul(bank[:, 2 * e8:3 * e8], C("ones"), RT[:, 1, :], start=False, stop=True)
            closed(pre, ("pos",), ins)

            def gather(half, free_from, pg):
                pe.wait_ge(S("e_pg"), pg)
                if half or free_from is not None:
                    pe.wait_ge(S("e_miscfree"), free_from)
                for c in range(4 * half, 4 * half + 4):
                    for tt in range(TT):
                        ins = nc.tensor.matmul(ps[7][:, (c % 4) * P:(c % 4 + 1) * P], H[:, tt, c * P:(c + 1) * P], PG[:, tt, :],
                                               start=(tt == 0), stop=(tt == TT - 1))
                        if tt == 0:
                            pay(ins)
                ins.then_inc(S("e_misc"), 1)

            for b in range(8):
                pe.wait_ge(pre.free[b], pre.uses[b])
            gather(0, None, 2)
            gather(1, 1, 2)
            pe.wait_ge(S("pad"), 5)
            for n in range(4):
                ins = nc.tensor.matmul(ps[4 + n // 2][:, (n % 2) * SEQ:(n % 2 + 1) * SEQ], PTX[:, 0:P], PTX, start=True, stop=True)
            ins.then_inc(S("e_used"), SPLIT)
            pe.wait_ge(S("routed"), 1)
            n_items = pe.value_load(nit[0:1, 0:1], min_val=EXPERTS, max_val=EXPERTS + 3)
            with pe.Fori(0, n_items) as i:
                at = {"j": 0}

                def three(bank, xh, xl, h, l, start, stop):
                    first = nc.tensor.matmul(bank, xh, h, start=start, stop=False)
                    nc.tensor.matmul(bank, xh, l, start=False, stop=False)
                    return first, nc.tensor.matmul(bank, xl, h, start=False, stop=stop)

                def half_unit():
                    h = at["j"]
                    at["j"] += 1
                    pe.wait_ge(S("split"), i * HALVES + (RAW + h + 1))
                    return half_of(wh, h % SPLIT), half_of(wl, h % SPLIT)

                def product(bank, n):
                    per = HALF // n
                    for part in range(DC // per):
                        h, l = (t.rearrange("p (c n) -> p c n", c=per) for t in half_unit())
                        for c in range(per):
                            k = part * per + c
                            first, ins = three(bank[:, 0:n], HTGH[:, k, :], HTGL[:, k, :], h[:, c, :], l[:, c, :],
                                               k == 0, k == DC - 1)
                            if k == 0:
                                pay(first)
                        if part < DC // per - 1:
                            ins.then_inc(S("e_used"), 1)
                    ins.then_inc(S("e_gu"), 1)
                    owed.append("e_used")

                def misc(r):
                    pe.wait_ge(S("e_miscfree"), i * 7 + (2 + r))

                def scatter(n):
                    misc((0, 2, 4, 5)[n])
                    if n == 0:
                        pe.wait_ge(S("e_ys"), i * 2 + 2)
                    for c in range(2):
                        ins = nc.tensor.matmul(ps[7][:, c * 256:(c + 1) * 256], PTX[:, (n // 2) * P:(n // 2 + 1) * P],
                                               YS[:, (n % 2) * 512 + c * 256:(n % 2) * 512 + (c + 1) * 256], start=True, stop=True)
                        if c == 0:
                            pay(ins)
                    ins.then_inc(S("e_misc"), 1)

                def transposes(s):
                    n = 4 if s < 5 else 2
                    pe.wait_ge(S("e_prod"), i * 6 + (s + 1))
                    for t in range(n):
                        ins = nc.tensor.transpose(ps[6][:, t * P:(t + 1) * P], PRD[:, s % 2, t * P:(t + 1) * P], ident)
                        if t == 0:
                            pay(ins)
                    ins.then_inc(S("e_tr"), 1)

                def down_step(s):
                    n = 4 if s < 5 else 2
                    pe.wait_ge(S("e_at"), i * 6 + (s + 1))
                    for part in range(n // 2):
                        h, l = (t.rearrange("p (f n) -> p f n", f=2) for t in half_unit())
                        for f in range(2):
                            t = 2 * part + f
                            for c in range(2):
                                cols = slice(c * 512, (c + 1) * 512)
                                first, ins = three(ps[4 + c][:, :], ATEH[:, s % 2, t * P:(t + 1) * P],
                                                   ATEL[:, s % 2, t * P:(t + 1) * P], h[:, f, cols], l[:, f, cols],
                                                   s == 0 and t == 0, s == 5 and t == n - 1)
                                if t == 0 and c == 0:
                                    pay(first)
                        ins.then_inc(S("e_used"), 1)

                pe.wait_ge(S("e_htg"), i + 1)
                for s in range(6):
                    product(ps[s % 2], 512 if s < 5 else 256)
                    if s < 4:
                        scatter(s)
                    if s == 4:
                        misc(6)
                        pe.wait_ge(S("e_px"), i * 2 + 2)
                        for tt in range(TT):
                            pay(nc.tensor.transpose(ps[7][:, tt * P:(tt + 1) * P], PX[:, tt, :], ident))
                        for tt in range(TT):
                            ins = nc.tensor.matmul(ps[7][:, SEQ:SEQ + 1], PX[:, tt, :], rt[:, 400 + tt:401 + tt],
                                                   start=(tt == 0), stop=(tt == TT - 1))
                        ins.then_inc(S("e_misc"), 1)
                    if s:
                        transposes(s - 1)
                    product(ps[2 + s % 2], 512 if s < 5 else 256)
                    if s < 2:
                        gather(s, i * 7 + (2 + 1 + 2 * s), i * 2 + 4)
                    if s:
                        down_step(s - 1)
                transposes(5)
                down_step(5)
            pe.wait_ge(S("e_ys"), n_items * 2 + 2)
            pe.wait_ge(S("e_miscfree"), n_items * 7 + 2)
            for n in range(4):
                nc.tensor.matmul(ps[4 + n][:, :], PTX[:, (n // 2) * P:(n // 2 + 1) * P], YS[:, (n % 2) * 512:(n % 2 + 1) * 512],
                                 start=True, stop=True).then_inc(S("last_full"), 1)
            pe.wait_ge(S("experts_done"), 1)
            pe.wait_ge(S("ld_bias"), 16)
            bank = opened(pe, post, ("hk",))
            ins = nc.tensor.matmul(bank[0:GH, 0:HK], vec[0:BUCKETS, VEC["relb"]:VEC["relb"] + GH], g1[0:BUCKETS, 0:HK], start=True, stop=True)
            closed(post, ("hk",), ins)
            norm_pe(pe, post, 5, 5)
            ht_ready(pe, 5)
            for name in ("q2", "k2"):
                w = unit().rearrange("p (c n) -> p c n", c=DC)
                for i in range(4):
                    ins = feature_tile(post, (name, i), lambda c, i=i: w[:, c, i * P:(i + 1) * P], HT)
                used()
            token_tiles(post, "v2", HT, halves=1)
            for name in (("q2", 3), ("k2", 3), ("v2", 1)):
                b, k = post.at[name]
                pe.wait_ge(post.free[b], k + 1)
            pe.wait_ge(S("q_ready"), DC + 4)
            pe.wait_ge(S("hk_in"), 16 * GH)
            attention_pe(post, 1, GH)
            pe.wait_ge(S("att_done"), 2)
            for u in range(3):
                w = unit().rearrange("p (c n) -> p c n", c=DC)
                for i in range(4):
                    ins = feature_tile(post, ("g", 4 * u + i), lambda c, i=i: w[:, c, i * P:(i + 1) * P], HT)
                used()
            token_tiles(post, "z", HT, halves=1)
            wab = nar[:, WAB:WAB + DC * 2 * GH].rearrange("p (c n) -> p c n", c=DC)
            bank = opened(pe, post, ("ab",))
            for tt in range(TT):
                for c in range(DC):
                    ins = nc.tensor.matmul(bank[:, tt * 16:(tt + 1) * 16], HT[:, c, tt * P:(tt + 1) * P], wab[:, c, :],
                                           start=(c == 0), stop=(c == DC - 1))
            closed(post, ("ab",), ins)
            pe.wait_ge(S("glog"), 1)
            bank = opened(pe, post, ("gcum",))
            for j, tri in enumerate(("tri64", "all64")):
                for tt in range(TT):
                    ins = nc.tensor.matmul(bank[:, (2 * j + tt) * GH:(2 * j + tt + 1) * GH], C(tri), GLOG[:, tt, :], start=True, stop=True)
            closed(post, ("gcum",), ins)
            pe.wait_ge(S("gcum_ready"), 1)
            bank = opened(pe, post, ("gT",))
            for tt in range(TT):
                nc.tensor.transpose(bank[0:GH, tt * P:(tt + 1) * P], GC[:, tt, :], ident)
            for c in range(4):
                last = (c % 2) * CHUNK + CHUNK - 1
                ins = nc.tensor.matmul(bank[:, SEQ + c * GH:SEQ + (c + 1) * GH], ident[:, last:last + 1].to_broadcast([P, P]),
                                       GC[:, c // 2, :], start=True, stop=True)
            closed(post, ("gT",), ins)
            for tt in range(TT):
                for j in range(3):
                    pe.wait_ge(S("g_silu"), 4 * j + 4)
                    if tt == 0 and j == 0:
                        pe.wait_ge(S("g_silu"), 12)
                    bank = opened(pe, post, ("tm", tt, j))
                    for c in range(4):
                        ins = nc.tensor.transpose(bank[:, c * P:(c + 1) * P], GF[:, 4 * j + c, tt * P:(tt + 1) * P], ident)
                    closed(post, ("tm", tt, j), ins)
            pe.wait_ge(S("tm_ready"), 2)
            pe.wait_ge(S("gc_ready"), 1)
            for tt in range(TT):
                for q in range(2):
                    for n, src in (("KT", KN[tt]), ("KBT", KB[:, tt, :]), ("QT", QN[tt]), ("QDT", QD[:, tt, :])):
                        bank = opened(pe, post, (n, tt, q))
                        for h in range(4):
                            ins = nc.tensor.transpose(bank[0:DH, h * P:(h + 1) * P], src[:, (4 * q + h) * DH:(4 * q + h + 1) * DH], ident)
                        closed(post, (n, tt, q), ins)
                for n in ("KT", "KBT", "QT", "QDT"):
                    b, k = post.at[(n, tt, 1)]
                    pe.wait_ge(post.free[b], k + 1)
                for q in range(2):
                    bank = opened(pe, post, ("DT", tt, q))
                    for h in range(4):
                        o = bank[:, h * P:(h + 1) * P]
                        nc.tensor.matmul(o, ident[0:GH, 4 * q + h:4 * q + h + 1].to_broadcast([GH, P]), GTR[:, tt * P:(tt + 1) * P],
                                         start=True, stop=False)
                        ins = nc.tensor.matmul(o, ident, C("blockdecay"), start=False, stop=True)
                    closed(post, ("DT", tt, q), ins)
                    for n, src in (("KK", KBTt), ("QK", QTt)):
                        bank = opened(pe, post, (n, tt, q))
                        for h in range(4):
                            ins = nc.tensor.matmul(bank[:, h * P:(h + 1) * P], KTt[:, 4 * q + h, :], src[:, 4 * q + h, :],
                                                   start=True, stop=True)
                        closed(post, (n, tt, q), ins)
                for lv in range(LEVELS):
                    pe.wait_ge(S("ci_ready"), tt * LEVELS + lv + 1)
                    if tt * LEVELS + lv:
                        pe.wait_ge(S("level"), tt * LEVELS + lv)
                    for q in range(2):
                        bank = opened(pe, post, ("Z", tt, lv, q))
                        for h in range(4 * q, 4 * q + 4):
                            ins = nc.tensor.matmul(bank[:, (h % 4) * P:(h % 4 + 1) * P], CI[:, h * P:(h + 1) * P], XI[:, h * P:(h + 1) * P],
                                                   start=True, stop=True)
                        closed(post, ("Z", tt, lv, q), ins)
                    for q in range(2):
                        b, k = post.at[("Z", tt, lv, q)]
                        pe.wait_ge(post.free[b], k + 1)
                        for n in ("XZ", "ZW"):
                            bank = opened(pe, post, (n, tt, lv, q))
                            for h in range(4 * q, 4 * q + 4):
                                sl = slice(h * P, (h + 1) * P)
                                lhs, rhs = (WI, ZI) if n == "XZ" else (ZI, WI)
                                ins = nc.tensor.matmul(bank[:, (h % 4) * P:(h % 4 + 1) * P], lhs[:, sl], rhs[:, sl], start=True, stop=True)
                            closed(post, (n, tt, lv, q), ins)
                pe.wait_ge(S("level"), (tt + 1) * LEVELS)
                bank = opened(pe, post, ("U", tt))
                for h in range(GH):
                    ins = nc.tensor.matmul(bank[:, h * DH:(h + 1) * DH], WI[:, h * P:(h + 1) * P], VB[:, tt, h * DH:(h + 1) * DH],
                                           start=True, stop=True)
                closed(post, ("U", tt), ins)
                for q in range(2):
                    bank = opened(pe, post, ("WT", tt, q))
                    for h in range(4 * q, 4 * q + 4):
                        ins = nc.tensor.matmul(bank[0:DH, (h % 4) * P:(h % 4 + 1) * P], RW[:, tt, h * DH:(h + 1) * DH],
                                               WI[:, h * P:(h + 1) * P], start=True, stop=True)
                    closed(post, ("WT", tt, q), ins)
            for tt in range(TT):
                b, k = post.at[("WT", tt, 1)]
                pe.wait_ge(post.free[b], k + 1)
                b, k = post.at[("U", tt)]
                pe.wait_ge(post.free[b], k + 1)
            for c in range(4):
                tt, b0 = c // 2, (c % 2) * CHUNK
                sl = slice(b0, b0 + CHUNK)
                pe.wait_ge(S("st_ready"), c + 1)
                bank = opened(pe, post, ("vn", c))
                for h in range(GH):
                    ins = nc.tensor.matmul(bank[sl, h * DH:(h + 1) * DH], WT[tt][:, h, sl], ST[:, h, :], start=True, stop=True)
                closed(post, ("vn", c), ins)
                bank = opened(pe, post, ("o", c))
                pe.wait_ge(S("vn_ready"), c + 1)
                for h in range(GH):
                    o = bank[sl, h * DH:(h + 1) * DH]
                    nc.tensor.matmul(o, QDT[:, h, c * CHUNK:(c + 1) * CHUNK], ST[:, h, :], start=True, stop=False)
                    ins = nc.tensor.matmul(o, ATG[:, tt, h, sl], VN[c % 2][:, h * DH:(h + 1) * DH], start=False, stop=True)
                closed(post, ("o", c), ins)
                bank = opened(pe, post, ("st", c))
                for h in range(GH):
                    ins = nc.tensor.matmul(bank[0:DH, h * DH:(h + 1) * DH], KD[:, tt, h * DH:(h + 1) * DH], VN[c % 2][:, h * DH:(h + 1) * DH],
                                           start=True, stop=True)
                closed(post, ("st", c), ins)
            for tt in range(TT):
                pe.wait_ge(S("og_ready"), tt + 1)
                bank = opened(pe, post, ("og", tt))
                for c in range(4):
                    ins = nc.tensor.transpose(bank[:, c * P:(c + 1) * P], OG[:, tt, c * P:(c + 1) * P], ident)
                closed(post, ("og", tt), ins)
            b, k = post.at[("og", 1)]
            pe.wait_ge(post.free[b], k + 1)
            token_tiles(post, "mix", F3c)
            norm_pe(pe, post, 7, 6)
            ht_ready(pe, 7)
            for u in range(8):
                w = unit().rearrange("p (c n) -> p c n", c=DC)
                for i in range(4):
                    ins = feature_tile(post, ("up", 4 * u + i), lambda c, i=i: w[:, c, i * P:(i + 1) * P], HT)
                used()
            pe.wait_ge(S("up_prod"), FT2)
            down(post, "mlp", AT, FT2)


def ktile(w):
    return w.reshape(-1, P, w.shape[1]).transpose(1, 0, 2)


def lay_out(inp):
    ws = np.zeros((POST0 + N_POST, P, UNIT), np.float32)
    n = 0

    def put(*parts):
        nonlocal n
        at = 0
        for a in parts:
            a = a.reshape(P, -1)
            ws[n, :, at:at + a.shape[1]] = a
            at += a.shape[1]
        n += 1

    def columns(w, width=512):
        w = ktile(w)
        for c in range(0, w.shape[2], width):
            put(w[:, :, c:c + width])

    def pairs(a, b):
        a, b = ktile(a), ktile(b)
        for c in range(0, a.shape[2], 256):
            put(np.concatenate([a[:, :, c:c + 256], b[:, :, c:c + 256]], axis=2))

    def rows(w):
        w = ktile(w)
        for f in range(0, w.shape[1], 4):
            put(w[:, f:f + 4, :])

    w_in = inp["conv_w_in"][0]
    pairs(w_in[:, :D], w_in[:, D:])
    columns(inp["conv_w_out"][0])
    pairs(inp["ffn_w_gate"][0], inp["ffn_w_up"][0])
    rows(inp["ffn_w_down"][0])
    columns(inp["w_q"][0])
    columns(inp["w_kvf"][:, :2 * D])
    columns(inp["w_o"][0])
    assert n == N_PRE
    for e in range(EXPERTS):
        g, u, d = (ktile(inp[k][0, e]) for k in ("moe_w_gate", "moe_w_up", "moe_w_down"))
        for s in range(6):
            sl = slice(512 * s, min(512 * (s + 1), FF))
            if s < 5:
                put(g[:, :, sl])
                put(u[:, :, sl])
            else:
                put(g[:, :, sl], u[:, :, sl])
            if s:
                put(d[:, 4 * s - 4:4 * s, :])
        put(d[:, 20:22, :])
    assert n == POST0
    w2 = inp["w_in_2"][0]
    columns(w2[:, :3 * ATT2 + 4 * ATT2])
    columns(inp["w_out_2"][0])
    columns(inp["w_up_2"][0])
    rows(inp["w_down_2"][0])
    assert n == POST0 + N_POST

    vec = np.zeros((P, N_VEC), np.float32)

    def cols(name, a):
        a = a.reshape(-1, P).T
        vec[:, VEC[name]:VEC[name] + a.shape[1]] = a

    for name, a in [("mix0", inp["mix_norm"][0]), ("ffn0", inp["ffn_norm"][0]), ("mix1", inp["mix_norm"][1]),
                    ("ffn1", inp["ffn_norm"][1]), ("kv", inp["kv_norm"]), ("b_in", inp["conv_b_in"][0]),
                    ("w_dw", inp["conv_w_dw"][0]), ("b_dw", inp["conv_b_dw"][0]), ("ln_g", inp["conv_ln_g"][0]),
                    ("ln_b", inp["conv_ln_b"][0]), ("pre_mix", inp["pre_mix_norm_2"][0]),
                    ("pre_mlp", inp["pre_mlp_norm_2"][0]), ("conv2", inp["conv_w_2"][0])]:
        cols(name, a)
    vec[0:HEADS, VEC["b_f"]] = inp["b_f"]
    vec[0:BUCKETS, VEC["relb"]:VEC["relb"] + GH] = inp["rel_bias_2"].T
    narrow = np.concatenate([ktile(w).reshape(P, -1) for w in
                             (inp["w_kvf"][:, 2 * D:], inp["router_w"][0], w2[:, 7 * ATT2:])], axis=1)
    const, bias = shape_constants()
    return {
        "x": np.ascontiguousarray(inp["x"][0]),
        "ws": ws,
        "const": const,
        "bias": bias,
        "vec": vec,
        "narrow": np.ascontiguousarray(narrow),
        "rows": np.concatenate([inp["router_b"][0], inp["A_log_2"][0], inp["dt_bias_2"][0], inp["gdn_norm_w_2"][0]]),
        "gains": np.stack([inp["conv_b_out"][0], inp["final_norm"], inp["post_mix_norm_2"][0],
                           inp["post_mlp_norm_2"][0]]),
    }


def kernel(**inputs):
    import concourse.bacc as bacc
    from concourse.bass_utils import run_bass_kernel_spmd

    arrays = lay_out({k: np.asarray(v) for k, v in inputs.items()})
    nc = bacc.Bacc("TRN2", target_bir_lowering=False, num_devices=1)
    dr = {k: nc.dram_tensor("in_" + k, a.shape, F32, kind="ExternalInput").ap() for k, a in arrays.items()}
    dr["scratch"] = nc.dram_tensor("scratch", (GH, HK), F32).ap()
    out = nc.dram_tensor("out", (SEQ, D), F32, kind="ExternalOutput").ap()
    build(nc, dr, out, DEBUG(nc) if DEBUG else None)
    r = run_bass_kernel_spmd(nc, [{"in_" + k: a for k, a in arrays.items()}], core_ids=[0])
    return r.results[0]["out"].reshape(1, SEQ, D)


DEBUG = None
```
